# Optimizing a Trainium2 kernel written in Bass

```python
import math
import jax, jax.numpy as jnp
from jax import lax
import numpy as np

D_MODEL = 1024
BATCH = 1
SEQ = 128
DEPTH = 4
DEC_BATCH = 1
DEC_SEQ = 512
PAST_LEN = 128

GRID_W = 64
N_MIXERS = 4
HEAD_DIM = 64
N_HEADS = D_MODEL // HEAD_DIM
N_KV = N_HEADS // 4
GQA_GROUP = N_HEADS // N_KV
DIFF_HEADS = D_MODEL // (2 * HEAD_DIM)
POOL_WINDOWS = (2, 4, 8, 16)
POOL_GROUPS = len(POOL_WINDOWS)
POOL_CH = D_MODEL // POOL_GROUPS
WINDOW = 128
Q_BLOCK = 128
D_FF = ((8 * D_MODEL // 3 + 127) // 128) * 128
CONV_W = 3
ROPE_THETA = 10000.0
EPS = 1e-6
NEG = -1e30
N_POOL = (DEPTH + 3) // 4
N_GQA = (DEPTH + 2) // 4
N_DIFF = (DEPTH + 1) // 4
N_WIN = DEPTH // 4

kernel_name = "hybrid_dit_prefix_ctx_step"

F32 = jnp.float32

def rmsnorm(x, g):
    xf = x.astype(F32)
    y = xf * lax.rsqrt(jnp.mean(xf * xf, axis=-1, keepdims=True) + EPS)
    return (y * g.astype(F32)).astype(x.dtype)

def modulation(cvec, w_mod, b_mod):
    m = jax.nn.silu(cvec) @ w_mod + b_mod
    return jnp.split(m, 6, axis=-1)

def modulate(h, shift, scale):
    return h * (1 + scale) + shift

def rope_tables(S):
    rows = S // GRID_W
    row = jnp.repeat(jnp.arange(rows), GRID_W).astype(F32)
    col = jnp.tile(jnp.arange(GRID_W), rows).astype(F32)
    half = HEAD_DIM // 2
    inv = ROPE_THETA ** (-jnp.arange(0, half, 2, dtype=F32) / half)
    ang = jnp.stack([row[:, None] * inv, col[:, None] * inv], axis=1)
    return jnp.cos(ang), jnp.sin(ang)

def apply_rope(x, cos, sin):
    shp = x.shape
    xa = x.astype(F32).reshape(shp[:-1] + (2, 2, HEAD_DIM // 4))
    x1, x2 = xa[..., 0, :], xa[..., 1, :]
    bshape = (shp[1],) + (1,) * (x.ndim - 3) + (2, HEAD_DIM // 4)
    cs, sn = cos.reshape(bshape), sin.reshape(bshape)
    out = jnp.stack([x1 * cs - x2 * sn, x2 * cs + x1 * sn], axis=-2)
    return out.reshape(shp).astype(x.dtype)

def pool_mix(h, w_pool, scale):
    B, S, D = h.shape
    hf = h.astype(F32)
    cs = jnp.concatenate([jnp.zeros((B, 1, D), F32), jnp.cumsum(hf, axis=1)], axis=1)
    t = jnp.arange(S)
    outs = []
    for g, w in enumerate(POOL_WINDOWS):
        lo = jnp.clip(t - w // 2, 0, S)
        hi = jnp.clip(t - w // 2 + w, 0, S)
        sl = slice(g * POOL_CH, (g + 1) * POOL_CH)
        csg = cs[:, :, sl]
        cnt = (hi - lo).astype(F32)[None, :, None]
        pooled = (csg[:, hi] - csg[:, lo]) / cnt - hf[:, :, sl]
        outs.append(pooled.astype(h.dtype) @ w_pool[g])
    return jnp.concatenate(outs, axis=-1) * scale

def conv_ffn(h, w_in, conv_w, conv_b, w_out):
    u = h @ w_in
    up = jnp.pad(u, ((0, 0), (1, 1), (0, 0)))
    uc = up[:, :-2] * conv_w[0] + up[:, 1:-1] * conv_w[1] + up[:, 2:] * conv_w[2] + conv_b
    a, b = jnp.split(uc, 2, axis=-1)
    return (jax.nn.silu(a) * b) @ w_out

def gqa_proj(h, w_qkv, qn, kn):
    B, S, _ = h.shape
    qkv = h @ w_qkv
    nq, nk = N_HEADS * HEAD_DIM, N_KV * HEAD_DIM
    q = qkv[..., :nq].reshape(B, S, N_HEADS, HEAD_DIM)
    k = qkv[..., nq:nq + nk].reshape(B, S, N_KV, HEAD_DIM)
    v = qkv[..., nq + nk:].reshape(B, S, N_KV, HEAD_DIM)
    return rmsnorm(q, qn), rmsnorm(k, kn), v

def gqa_attend(q, k, v, sink=None):
    B, S, H, Dh = q.shape
    nb = S // Q_BLOCK
    qb = q.reshape(B, nb, Q_BLOCK, N_KV, GQA_GROUP, Dh).transpose(1, 0, 2, 3, 4, 5)
    scale = Dh ** -0.5

    def one(qblk):
        s = jnp.einsum('bqkgd,blkd->bkgql', qblk, k).astype(F32) * scale
        if sink is not None:
            col = jnp.broadcast_to(sink.astype(F32).reshape(1, N_KV, GQA_GROUP, 1, 1), s.shape[:-1] + (1,))
            p = jax.nn.softmax(jnp.concatenate([s, col], axis=-1), axis=-1)[..., :-1]
        else:
            p = jax.nn.softmax(s, axis=-1)
        return jnp.einsum('bkgql,blkd->bqkgd', p.astype(v.dtype), v)

    o = lax.map(one, qb)
    return o.transpose(1, 0, 2, 3, 4, 5).reshape(B, S, H * Dh)

def window_attend(q, k_lat, v_lat, k_ctx, v_ctx, sink):
    B, S, H, Dh = q.shape
    nb = S // Q_BLOCK
    scale = Dh ** -0.5

    def band(a):
        ap = jnp.pad(a, ((0, 0), (WINDOW, WINDOW), (0, 0), (0, 0)))
        ab = ap.reshape(B, nb + 2, Q_BLOCK, N_KV, Dh)
        return jnp.concatenate([ab[:, :-2], ab[:, 1:-1], ab[:, 2:]], axis=2)

    kw, vw = band(k_lat), band(v_lat)
    qb = q.reshape(B, nb, Q_BLOCK, N_KV, GQA_GROUP, Dh)
    s_loc = jnp.einsum('bnqkgd,bnlkd->bnkgql', qb, kw).astype(F32) * scale
    s_ctx = jnp.einsum('bnqkgd,blkd->bnkgql', qb, k_ctx).astype(F32) * scale
    qi = jnp.arange(Q_BLOCK)[:, None]
    kj = jnp.arange(3 * Q_BLOCK)[None, :]
    kpos = jnp.arange(nb)[:, None, None] * Q_BLOCK - Q_BLOCK + kj
    valid = (jnp.abs(kj - Q_BLOCK - qi) <= WINDOW)[None] & (kpos >= 0) & (kpos < S)
    s_loc = jnp.where(valid[None, :, None, None], s_loc, NEG)
    col = jnp.broadcast_to(sink.astype(F32).reshape(1, 1, N_KV, GQA_GROUP, 1, 1), s_loc.shape[:-1] + (1,))
    p = jax.nn.softmax(jnp.concatenate([s_loc, s_ctx, col], axis=-1), axis=-1)
    nl = 3 * Q_BLOCK
    p_loc = p[..., :nl].astype(v_lat.dtype)
    p_ctx = p[..., nl:-1].astype(v_lat.dtype)
    o = jnp.einsum('bnkgql,bnlkd->bnqkgd', p_loc, vw) + jnp.einsum('bnkgql,blkd->bnqkgd', p_ctx, v_ctx)
    return o.reshape(B, S, H * Dh)

def diff_proj(h, w_qkv, qn, kn):
    B, S, _ = h.shape
    qkv = h @ w_qkv
    q = qkv[..., :D_MODEL].reshape(B, S, DIFF_HEADS, 2, HEAD_DIM)
    k = qkv[..., D_MODEL:2 * D_MODEL].reshape(B, S, DIFF_HEADS, 2, HEAD_DIM)
    v = qkv[..., 2 * D_MODEL:].reshape(B, S, DIFF_HEADS, 2 * HEAD_DIM)
    return rmsnorm(q, qn), rmsnorm(k, kn), v

def diff_attend(q, k, v, lam):
    B, S, H, _, Dh = q.shape
    nb = S // Q_BLOCK
    qb = q.reshape(B, nb, Q_BLOCK, H, 2, Dh).transpose(1, 0, 2, 3, 4, 5)
    scale = Dh ** -0.5

    def one(qblk):
        s = jnp.einsum('bqhcd,blhcd->bhcql', qblk, k).astype(F32) * scale
        p = jax.nn.softmax(s, axis=-1)
        pd = p[:, :, 0] - lam * p[:, :, 1]
        return jnp.einsum('bhql,blhe->bqhe', pd.astype(v.dtype), v)

    o = lax.map(one, qb)
    return o.transpose(1, 0, 2, 3, 4).reshape(B, S, H, 2 * Dh)

def diff_lambda(lq1, lk1, lq2, lk2, lambda_init):
    return (jnp.exp(jnp.sum(lq1.astype(F32) * lk1.astype(F32)))
            - jnp.exp(jnp.sum(lq2.astype(F32) * lk2.astype(F32))) + lambda_init)

def diff_out(o, sub_g, lambda_init, w_o):
    B, S = o.shape[:2]
    o = rmsnorm(o, sub_g) * (1.0 - lambda_init)
    return o.reshape(B, S, D_MODEL) @ w_o

def setup_inputs(seed: int = 0) -> dict:
    key = jax.random.key(seed)
    ks = iter(jax.random.split(key, 64))
    nrm = lambda shape, s=1.0: jax.random.normal(next(ks), shape, F32) * s
    D, F = D_MODEL, D_FF
    return {
        "x_prompt": nrm((BATCH, SEQ, D)),
        "x_sample": nrm((DEC_BATCH, DEC_SEQ, D)),
        "cache_gqa_k": nrm((DEC_BATCH, N_GQA, PAST_LEN, N_KV, HEAD_DIM)),
        "cache_gqa_v": nrm((DEC_BATCH, N_GQA, PAST_LEN, N_KV, HEAD_DIM)),
        "cache_diff_k": nrm((DEC_BATCH, N_DIFF, PAST_LEN, DIFF_HEADS, 2, HEAD_DIM)),
        "cache_diff_v": nrm((DEC_BATCH, N_DIFF, PAST_LEN, DIFF_HEADS, 2 * HEAD_DIM)),
        "cache_win_k": nrm((DEC_BATCH, N_WIN, PAST_LEN, N_KV, HEAD_DIM)),
        "cache_win_v": nrm((DEC_BATCH, N_WIN, PAST_LEN, N_KV, HEAD_DIM)),
        "c": nrm((DEC_BATCH, D)),
        "c_ctx": nrm((D,)),
        "norm1_g": 1.0 + nrm((DEPTH, D), 0.05),
        "norm2_g": 1.0 + nrm((DEPTH, D), 0.05),
        "w_mod": nrm((DEPTH, D, 6 * D), 0.5 * D ** -0.5),
        "b_mod": nrm((DEPTH, 6 * D), 0.02),
        "ffn_w_in": nrm((DEPTH, D, 2 * F), D ** -0.5),
        "ffn_conv_w": nrm((DEPTH, CONV_W, 2 * F), CONV_W ** -0.5),
        "ffn_conv_b": nrm((DEPTH, 2 * F), 0.02),
        "ffn_w_out": nrm((DEPTH, F, D), F ** -0.5),
        "pool_w": nrm((N_POOL, POOL_GROUPS, POOL_CH, POOL_CH), POOL_CH ** -0.5),
        "pool_scale": 1.0 + nrm((N_POOL, D), 0.1),
        "gqa_w_qkv": nrm((N_GQA, D, (N_HEADS + 2 * N_KV) * HEAD_DIM), D ** -0.5),
        "gqa_q_norm": 1.0 + nrm((N_GQA, HEAD_DIM), 0.05),
        "gqa_k_norm": 1.0 + nrm((N_GQA, HEAD_DIM), 0.05),
        "gqa_w_o": nrm((N_GQA, N_HEADS * HEAD_DIM, D), (N_HEADS * HEAD_DIM) ** -0.5),
        "diff_w_qkv": nrm((N_DIFF, D, 3 * D), D ** -0.5),
        "diff_q_norm": 1.0 + nrm((N_DIFF, HEAD_DIM), 0.05),
        "diff_k_norm": 1.0 + nrm((N_DIFF, HEAD_DIM), 0.05),
        "diff_lambda_q1": nrm((N_DIFF, HEAD_DIM), 0.1),
        "diff_lambda_k1": nrm((N_DIFF, HEAD_DIM), 0.1),
        "diff_lambda_q2": nrm((N_DIFF, HEAD_DIM), 0.1),
        "diff_lambda_k2": nrm((N_DIFF, HEAD_DIM), 0.1),
        "diff_sub_norm": 1.0 + nrm((N_DIFF, 2 * HEAD_DIM), 0.05),
        "diff_w_o": nrm((N_DIFF, D, D), D ** -0.5),
        "win_w_qkv": nrm((N_WIN, D, (N_HEADS + 2 * N_KV) * HEAD_DIM), D ** -0.5),
        "win_q_norm": 1.0 + nrm((N_WIN, HEAD_DIM), 0.05),
        "win_k_norm": 1.0 + nrm((N_WIN, HEAD_DIM), 0.05),
        "win_sink": nrm((N_WIN, N_HEADS), 0.5),
        "win_w_o": nrm((N_WIN, N_HEADS * HEAD_DIM, D), (N_HEADS * HEAD_DIM) ** -0.5),
    }

def reference(x_prompt, x_sample, cache_gqa_k, cache_gqa_v, cache_diff_k, cache_diff_v,
              cache_win_k, cache_win_v, c, c_ctx, norm1_g, norm2_g, w_mod, b_mod,
              ffn_w_in, ffn_conv_w, ffn_conv_b, ffn_w_out, pool_w, pool_scale,
              gqa_w_qkv, gqa_q_norm, gqa_k_norm, gqa_w_o,
              diff_w_qkv, diff_q_norm, diff_k_norm, diff_lambda_q1, diff_lambda_k1,
              diff_lambda_q2, diff_lambda_k2, diff_sub_norm, diff_w_o,
              win_w_qkv, win_q_norm, win_k_norm, win_sink, win_w_o):
    xp, xs = x_prompt, x_sample
    cos, sin = rope_tables(xs.shape[1])
    gk, gv, dk, dv, wk, wv = [], [], [], [], [], []
    for i in range(DEPTH):
        m, j = i % N_MIXERS, i // N_MIXERS
        p_sh1, p_sc1, p_g1, p_sh2, p_sc2, p_g2 = modulation(c_ctx, w_mod[i], b_mod[i])
        s_sh1, s_sc1, s_g1, s_sh2, s_sc2, s_g2 = [t[:, None, :] for t in modulation(c, w_mod[i], b_mod[i])]
        hp = modulate(rmsnorm(xp, norm1_g[i]), p_sh1, p_sc1)
        hs = modulate(rmsnorm(xs, norm1_g[i]), s_sh1, s_sc1)
        if m == 0:
            op = pool_mix(hp, pool_w[j], pool_scale[j])
            os_ = pool_mix(hs, pool_w[j], pool_scale[j])
        elif m == 1:
            q, k, v = gqa_proj(hp, gqa_w_qkv[j], gqa_q_norm[j], gqa_k_norm[j])
            gk.append(k); gv.append(v)
            op = gqa_attend(q, k, v) @ gqa_w_o[j]
            q, k, v = gqa_proj(hs, gqa_w_qkv[j], gqa_q_norm[j], gqa_k_norm[j])
            q, k = apply_rope(q, cos, sin), apply_rope(k, cos, sin)
            k_all = jnp.concatenate([cache_gqa_k[:, j], k], axis=1)
            v_all = jnp.concatenate([cache_gqa_v[:, j], v], axis=1)
            os_ = gqa_attend(q, k_all, v_all) @ gqa_w_o[j]
        elif m == 2:
            lam_init = 0.8 - 0.6 * math.exp(-0.3 * i)
            lam = diff_lambda(diff_lambda_q1[j], diff_lambda_k1[j], diff_lambda_q2[j], diff_lambda_k2[j], lam_init)
            q, k, v = diff_proj(hp, diff_w_qkv[j], diff_q_norm[j], diff_k_norm[j])
            dk.append(k); dv.append(v)
            op = diff_out(diff_attend(q, k, v, lam), diff_sub_norm[j], lam_init, diff_w_o[j])
            q, k, v = diff_proj(hs, diff_w_qkv[j], diff_q_norm[j], diff_k_norm[j])
            q, k = apply_rope(q, cos, sin), apply_rope(k, cos, sin)
            k_all = jnp.concatenate([cache_diff_k[:, j], k], axis=1)
            v_all = jnp.concatenate([cache_diff_v[:, j], v], axis=1)
            os_ = diff_out(diff_attend(q, k_all, v_all, lam), diff_sub_norm[j], lam_init, diff_w_o[j])
        else:
            q, k, v = gqa_proj(hp, win_w_qkv[j], win_q_norm[j], win_k_norm[j])
            wk.append(k); wv.append(v)
            op = gqa_attend(q, k, v, win_sink[j]) @ win_w_o[j]
            q, k, v = gqa_proj(hs, win_w_qkv[j], win_q_norm[j], win_k_norm[j])
            q, k = apply_rope(q, cos, sin), apply_rope(k, cos, sin)
            os_ = window_attend(q, k, v, cache_win_k[:, j], cache_win_v[:, j], win_sink[j]) @ win_w_o[j]
        xp = xp + p_g1 * op
        xs = xs + s_g1 * os_
        hp = modulate(rmsnorm(xp, norm2_g[i]), p_sh2, p_sc2)
        hs = modulate(rmsnorm(xs, norm2_g[i]), s_sh2, s_sc2)
        xp = xp + p_g2 * conv_ffn(hp, ffn_w_in[i], ffn_conv_w[i], ffn_conv_b[i], ffn_w_out[i])
        xs = xs + s_g2 * conv_ffn(hs, ffn_w_in[i], ffn_conv_w[i], ffn_conv_b[i], ffn_w_out[i])
    new_gqa_k = jnp.stack(gk, axis=1)
    new_gqa_v = jnp.stack(gv, axis=1)
    new_diff_k = jnp.stack(dk, axis=1)
    new_diff_v = jnp.stack(dv, axis=1)
    new_win_k = jnp.stack(wk, axis=1)
    new_win_v = jnp.stack(wv, axis=1)
    return (xp, xs, new_gqa_k, new_gqa_v, new_diff_k, new_diff_v, new_win_k, new_win_v)


_drawn_inputs = setup_inputs


def setup_inputs(seed=0):
    import zlib

    import numpy as np

    out = dict(_drawn_inputs(seed))
    spreads = {}
    factors = {'cache_gqa_k': 8.0,
     'cache_gqa_v': 6.144,
     'cache_win_k': 4.765,
     'cache_win_v': 3.828,
     'ffn_conv_b': 5.329,
     'gqa_q_norm': 8.0,
     'diff_q_norm': 8.0,
     'diff_lambda_q2': 2.817,
     'diff_lambda_k2': 189.0,
     'diff_sub_norm': 7.711,
     'win_q_norm': 8.0,
     'win_sink': 64.0}
    for name, (base, spread) in spreads.items():
        noise = np.random.default_rng([zlib.crc32(name.encode()), seed]).standard_normal(out[name].shape)
        drawn = base * np.exp(spread * noise) if base else spread * noise
        out[name] = __import__('jax').numpy.asarray(drawn.astype(out[name].dtype))
    for name, factor in factors.items():
        out[name] = (out[name] * factor).astype(out[name].dtype)
    return out
```

```python
import math
from contextlib import ExitStack

import numpy as np
import concourse.bass as bass
from concourse import mybir

F32 = mybir.dt.float32
F32R = mybir.dt.float32r
ALU = mybir.AluOpType
ACT = mybir.ActivationFunctionType
AX_X = mybir.AxisListType.X
ds = bass.ds

P = 128
D_MODEL = 1024
SEQ = 128
DEC_SEQ = 512
PAST = 128
DEPTH = 4
GRID_W = 64
DH = 64
HEADS = 16
KV_HEADS = 4
GROUP = HEADS // KV_HEADS
DIFF_HEADS = 8
POOL_WINDOWS = (2, 4, 8, 16)
D_FF = 2816
THETA = 10000.0
EPS = 1e-6
NEG = -1e30
SCALE = DH ** -0.5

KT = D_MODEL // P
NT = (SEQ + DEC_SEQ) // P
CTX0, LAT0 = 1, SEQ + 2
COLS = SEQ + DEC_SEQ + 4
HALF = COLS // 2
BANK = 512
UNITS = 8
UNIT = 512
FF_TILES = D_FF // P
ITERS = FF_TILES // 2
FIRST_PASSES = 4
MOD_PASSES = 12
KEY_TILES = NT + 1
CACHE_TILE = NT

MIX_CHUNKS = [1, 5, 8, 5]
QKV_CHUNKS = [0, 3, 6, 3]
FIRST_CHUNK = [sum(MIX_CHUNKS[:l]) + ITERS * l for l in range(DEPTH)]
FFN_CHUNK = [FIRST_CHUNK[l] + MIX_CHUNKS[l] for l in range(DEPTH)]
N_CHUNKS = FFN_CHUNK[-1] + ITERS

V_BMOD, V_N1, V_N2, V_CONV = 0, 48, 56, 64
V_LAYER = V_CONV + ITERS * 4 * 4
V_POOL = DEPTH * V_LAYER
V_COND = V_POOL + KT
V_SUM = V_COND + 2 * KT
V_ALL = V_SUM + 2
R_QN, R_KN, R_SUB, R_LAM, R_SINK = 0, 3 * DH, 6 * DH, 8 * DH, 12 * DH
R_ALL = R_SINK + HEADS
MOD_SH1, MOD_SC1, MOD_G1, MOD_SH2, MOD_SC2, MOD_G2 = (8 * i for i in range(6))

B_XT = 16512
B_H = B_XT + 4 * KT * COLS
B_W = B_H + 2 * 4 * KT * COLS
B_WO = B_W + 3 * 4 * UNITS * UNIT
B_N = B_WO + 3 * 4 * 2 * D_MODEL
B_C = B_N + 4 * NT * 3 * D_MODEL


def tile_col(j):
    return CTX0 if j == 0 else LAT0 + (j - 1) * P


def lam_init(layer):
    return 0.8 - 0.6 * math.exp(-0.3 * layer)


class Steps:

    def __init__(self, eng, sem):
        self.eng, self.sem, self.n, self.loop = eng, sem, 0, 0

    def __call__(self, ins):
        ins.then_inc(self.sem, 1)
        self.n += 1

    def wait(self):
        self.eng.wait_ge(self.sem, self.loop + self.n)


def band_tiles(j):
    return list(range(max(1, j - 1), min(NT - 1, j + 1) + 1))


def program(nc, t):
    with ExitStack() as ctx:
        place = [B_C]

        def at(name, shape, dtype, offset):
            return nc.alloc_sbuf_tensor_at(name, shape, dtype, offset=offset)

        def const(name, shape, dtype=F32):
            size = 4 * int(np.prod(shape[1:]))
            place[0] += -place[0] % 32
            place[0] += size
            return at(name, shape, dtype, place[0] - size)

        def sem(name):
            return ctx.enter_context(nc.semaphore(name))

        def sems(name, n):
            return [sem(f"{name}{i}") for i in range(n)]

        def att_sems(name, layers=(1, 2, 3)):
            return {l: sem(f"{name}{l}") for l in layers}

        xT = at("xT", [P, KT, COLS], F32, B_XT)
        h_hi = at("h_hi", [P, KT, COLS], F32R, B_H)
        h_lo = at("h_lo", [P, KT, COLS], F32R, B_H + 4 * KT * COLS)
        W = 4 * UNITS * UNIT
        w_stage = at("w_stage", [P, UNITS, UNIT], F32, B_W)
        w_hi = at("w_hi", [P, UNITS, UNIT], F32R, B_W + W)
        w_lo = at("w_lo", [P, UNITS, UNIT], F32R, B_W + 2 * W)
        WO = 4 * 2 * D_MODEL
        wo_stage = at("wo_stage", [P, 2, D_MODEL], F32, B_WO)
        wo_hi = at("wo_hi", [P, 2, D_MODEL], F32R, B_WO + WO)
        wo_lo = at("wo_lo", [P, 2, D_MODEL], F32R, B_WO + 2 * WO)
        M = 4 * 2 * KT * 2 * P
        m_stage = [at(f"m_stage{i}", [P, 2, KT, 2 * P], F32, B_N + i * M) for i in range(2)]
        C = 4 * COLS + -4 * COLS % 32
        u_raw = [at(f"u_raw{i}", [P, COLS], F32, B_N + M + i * C) for i in range(2)]
        conv = [at(f"conv{i}", [P, COLS], F32, B_N + M + (2 + i) * C) for i in range(2)]
        g_hi = at("g_hi", [P, 2, COLS], F32R, B_N + M + 4 * C)
        g_lo = at("g_lo", [P, 2, COLS], F32R, B_N + M + 6 * C)
        B_NORM = B_N + M + 8 * C
        sq_sum = at("sq_sum", [P, COLS], F32, B_NORM)
        sq = [at(f"sq{i}", [P, COLS], F32, B_NORM + (1 + i) * C) for i in range(2)]
        xs = [at(f"xs{i}", [P, COLS], F32, B_NORM + (3 + i) * C) for i in range(2)]
        rstd_rows = at("rstd_rows", [P, NT, P], F32, B_NORM + 5 * C)
        mod_rows = at("mod_rows", [P, 4, P], F32, B_NORM + 5 * C + 4 * NT * P)
        assert B_NORM + 5 * C + 4 * (NT + 4) * P <= B_C
        qkv = {3: at("qkv", [P, NT, 3 * UNIT], F32, B_N), 6: at("qkv_d", [P, NT, 6 * UNIT], F32, B_N)}
        PAD = 16
        PC = 3 * PAD + SEQ + DEC_SEQ
        inv_count = at("inv_count", [P, 4, SEQ + DEC_SEQ], F32, B_WO)
        hp = [at(f"hp{i}", [P, PC], F32, B_WO + 4 * 4 * (SEQ + DEC_SEQ) + i * 4 * PC) for i in range(3)]
        rope_raw = at("rope_raw", [P, 2, NT - 1, DH], F32, B_WO)
        qkv_sq = [at(f"qkv_sq{i}", [P, UNIT], F32, B_WO + 8192 + i * 2048) for i in range(2)]
        rope_a = at("rope_a", [P, UNIT], F32, B_WO + 12288)
        rope_b = at("rope_b", [P, UNIT], F32, B_WO + 14336)
        rope_cos = at("rope_cos", [P, 2, NT - 1, DH], F32, B_WO + 16384)
        rope_sin = at("rope_sin", [P, 2, NT - 1, DH], F32, B_WO + 18432)
        mask_raw = at("mask_raw", [P, 2, P], F32, B_WO + 20480)
        VB = B_WO + 6144
        v_hi = at("v_hi", [P, KEY_TILES, 3 * DH], F32R, VB)
        v_lo = at("v_lo", [P, KEY_TILES, 3 * DH], F32R, VB + 4608)
        vd_hi = [at("vd_hi0", [P, KEY_TILES, P], F32R, VB), at("vd_hi1", [P, KEY_TILES, P], F32R, B_W + 13312)]
        vd_lo = [at("vd_lo0", [P, KEY_TILES, P], F32R, VB + 3072), at("vd_lo1", [P, KEY_TILES, P], F32R, VB + 15360)]
        probs = [at(f"probs{i}", [P, 5 * P], F32, VB + 9216 + i * 2560) for i in range(2)]
        k_cache = [at(f"k_cache{i}", [P, DH], F32, VB + 14336 + i * 256) for i in range(2)]
        v_cache = [at(f"v_cache{i}", [P, DH], F32, VB + 14848 + i * 256) for i in range(2)]
        probs_d = [[at(f"probs_d{i}{m}", [P, 5 * P], F32, (VB + 6144 if i == 0 else B_W + 8192) + m * 2560)
                    for m in range(2)] for i in range(2)]
        out_d = at("out_d", [P, NT, P], F32, VB + 11264)
        k_cache_d = [at(f"k_cache_d{i}", [P, P], F32, VB + 13824 + i * 512) for i in range(2)]
        v_cache_d = [at("v_cache_d0", [P, P], F32, VB + 14848), const("v_cache_d1", [P, P])]
        B_A = B_W + W
        key_hi = [at(f"key_hi{i}", [P, KEY_TILES * P], F32R, (B_A, B_WO)[i]) for i in range(2)]
        key_lo = [at(f"key_lo{i}", [P, KEY_TILES * P], F32R, (B_A, B_WO)[i] + 3072) for i in range(2)]
        query = [at(f"query{i}", [P, NT * P], F32R, B_A + 6144 + i * 2560) for i in range(2)]
        PT = 4 * NT * 3 * UNIT + B_N
        pt_hi = [at(f"pt_hi{i}", [P, NT, 4 * P], F32R, (B_A + 11264, PT)[i]) for i in range(2)]
        pt_lo = [at(f"pt_lo{i}", [P, NT, 4 * P], F32R, (B_A + 21504, PT + 10240)[i]) for i in range(2)]
        ptc = [at(f"ptc{i}", [P, 2, P], F32R, PT + 20480 + i * 1024) for i in range(4)]
        assert PT + 24576 <= B_C
        KD = (B_A, B_A + 6144, B_WO)
        keyd_hi = [at(f"keyd_hi{i}", [P, KEY_TILES * P], F32R, KD[i]) for i in range(3)]
        keyd_lo = [at(f"keyd_lo{i}", [P, KEY_TILES * P], F32R, KD[i] + 3072) for i in range(3)]
        queryd = [[at(f"queryd{i}{m}", [P, NT * P], F32R, B_A + 12288 + (2 * i + m) * 2560)
                   for m in range(2)] for i in range(2)]
        ptd_hi = [at(f"ptd_hi{i}", [P, 5, P], F32R, B_A + 22528 + i * 5120) for i in range(2)]
        ptd_lo = [at(f"ptd_lo{i}", [P, 5, P], F32R, B_A + 25088 + i * 5120) for i in range(2)]
        ident = const("ident_sb", [P, P])
        ident_r = const("ident_r", [P, P], F32R)
        mask_r = const("mask_r", [P, 2, P], F32R)
        vec = const("vec_sb", [P, V_ALL])
        row = const("row_sb", [P, R_ALL])
        ones2 = const("ones2", [P, 2])
        minus_half = const("minus_half", [P, HEADS])
        cond = const("cond", [P, KT, 32])
        mod = [const(f"mod{i}", [P, 48, 2]) for i in range(2)]
        mod_a = const("mod_a", [P, KT, 2])
        pool_gate = const("pool_gate", [P, KT, 2])
        ms = const("ms", [P, NT])
        rs = const("rs", [P, NT])
        qms = [const(f"qms{i}", [P, 8]) for i in range(2)]
        qrs = [const(f"qrs{i}", [P, 8]) for i in range(2)]
        sub_g = const("sub_g", [P, P])
        out_sq = [const(f"out_sq{i}", [P, NT]) for i in range(2)]
        out_c = [const(f"out_c{i}", [P, P]) for i in range(2)]
        nsink = const("nsink", [P, HEADS])
        top = [const(f"top{i}", [P, 2]) for i in range(2)]
        shift = [const(f"shift{i}", [P, 2]) for i in range(2)]
        total = [const(f"total{i}", [P, 2]) for i in range(2)]
        sink_e = [const(f"sink_e{i}", [P, 1]) for i in range(2)]
        norm = [const(f"norm{i}", [P, 2]) for i in range(2)]
        lam = const("lam", [P, 4])
        lam_tmp = const("lam_tmp", [P, DH])
        mark = const("mark", [P, 8])
        assert place[0] <= nc.sbuf_usable_end, (place[0], nc.sbuf_usable_end)

        psA = ctx.enter_context(nc.psum_tensor("psA", [P, 4, BANK], F32))
        psB = ctx.enter_context(nc.psum_tensor("psB", [P, 4, BANK], F32))
        MOD_AT = 400

        s_small = sem("small_loaded")
        s_x = sem("x_loaded")
        s_w = sems("w_loaded", 2)
        s_wo = sem("wo_loaded")
        s_m = [sems("m_loaded_a", 2), sems("m_loaded_b", 2)]
        s_rope = sem("rope_loaded")
        s_cache = sems("cache_loaded", 2)
        s_kv_out = sem("kv_stored")
        s_y = sem("y_stored")
        s_count = sem("inv_count_loaded")
        s_mask = sem("mask_loaded")
        s_act = sem("act_steps")
        s_dve = sem("dve_steps")
        s_pool = sem("pool_steps")
        s_const = sem("consts_ready")
        s_cond = sem("cond_ready")
        s_whi = sem("w_hi_ready")
        s_wlo = sem("w_lo_ready")
        s_wused = sem("w_used")
        s_wohi = sem("wo_hi_ready")
        s_wolo = sem("wo_lo_ready")
        s_mraw = sem("mod_rows_computed")
        s_mrows = sem("mod_rows_copied")
        s_mod = sem("mod_computed")
        s_modok = sem("mod_ready")
        s_sq = sem("squares_ready")
        s_sqsum = sem("squares_added")
        s_stat = sem("norm_sums_ready")
        s_ms = sem("norm_means_ready")
        s_rs = sem("norm_rstd_ready")
        s_rows = sem("rstd_rows_ready")
        s_bc = sem("rstd_broadcast")
        s_xs = sem("x_scaled")
        s_hhi = sem("h_hi_ready")
        s_h = sem("h_ready")
        s_u = sems("u_evacuated", DEPTH)
        s_conv = sems("conv_done", DEPTH)
        s_silu = sems("silu_done", DEPTH)
        s_gate = sems("gate_done", DEPTH)
        s_ghi = sems("g_hi_ready", DEPTH)
        s_g = sems("g_ready", DEPTH)
        s_o = sems("ffn_out_computed", DEPTH)
        s_oadd = sems("ffn_out_added", DEPTH)
        s_mx = {0: sem("pool_out_computed")}
        s_mxadd = sems("mix_out_added", DEPTH)
        s_pooled = sem("pooled_ready")
        s_pooled_hi = sem("pooled_hi_ready")
        s_pool32 = sem("pooled_f32_ready")
        s_qp = att_sems("qkv_computed")
        s_qe = att_sems("qkv_evacuated")
        s_qms = att_sems("qk_means_ready")
        s_qrs = att_sems("qk_rstd_ready")
        s_qkv = sem("qkv_ready")
        s_vlo = att_sems("v_ready")
        s_vhi = att_sems("v_hi_ready")
        s_t = att_sems("transposed")
        s_ta = att_sems("t_taken_act")
        s_td = att_sems("t_taken_dve")
        s_s = att_sems("scores_ready")
        s_top = att_sems("shift_ready")
        s_e = att_sems("exp_done")
        s_p = att_sems("probs_ready")
        s_pv = att_sems("pv_done")
        s_ohi = att_sems("att_hi_ready")
        s_att = att_sems("att_ready")
        s_vzero = sem("value_pads_ready")
        s_lam = sem("lambda_sums_ready")
        s_lame = sem("lambda_exps_ready")
        s_osqa = sem("sub_squares_computed")
        s_oms = sem("sub_means_ready")
        s_ors = sem("sub_rstd_ready")
        s_on = sem("sub_normed")

        block = ctx.enter_context(nc.Block())

        def vcol(c, n=1):
            return vec[:, c:c + n] if isinstance(c, int) else vec[:, ds(c, n)]

        def wused_after(cg, units):
            return UNITS * cg + units

        def n_keys(layer, j):
            return P if j == 0 else (1 + len(band_tiles(j))) * P if layer == 3 else NT * P

        def split(n):
            return [(0, n)] if n <= 4 else [(0, 3), (3, n - 3)]

        def t_uses(layer):
            uses = []
            heads = DIFF_HEADS if layer == 2 else HEADS
            units = [(h, j) for h in range(heads) for j in range(NT)]

            def add(who, tiles, *key):
                uses.extend([((*key, i), who) for i in range(len(split(tiles)))])

            def prep(*a):
                add("ad", KEY_TILES, "k", *a)
                add("ad", NT, "q", *a)

            if layer == 2:
                prep(0, 0)
                prep(0, 1)
            else:
                prep(0)
            for u in range(len(units) + 3):
                h, j = units[u] if u < len(units) else (heads, u - len(units))
                if layer == 2 and u >= 3 and units[u - 3][1] == 0:
                    add("a", 1, "c", units[u - 3][0])
                if 1 <= u <= len(units):
                    add("ad", n_keys(layer, units[u - 1][1]) // P, "p", *units[u - 1])
                if layer == 2:
                    if j == 0 and h > 1:
                        uses.extend([(("o", h - 2, i), "ad") for i in range(2)])
                    if j in (2, 3) and h + 1 < heads:
                        prep(h + 1, j - 2)
                elif h < heads:
                    if j == 1 and h % GROUP == GROUP - 1 and h + 1 < heads:
                        add("ad", KEY_TILES, "k", h // GROUP + 1)
                    if j == 2 and h and h % 2 == 0:
                        add("ad", 1, "c", h - 1)
                    if j == 2 and h + 1 < heads:
                        add("ad", NT, "q", h + 1)
            if layer == 2:
                uses.extend([(("o", heads - 1, i), "ad") for i in range(2)])
            else:
                add("ad", 1, "c", heads - 1)
            table, counts = {}, [(0, 0)] * 3
            a = d = 0
            for i, (key, who) in enumerate(uses):
                table[key] = (i, a, d, counts[i % 3])
                a += "a" in who
                d += "d" in who
                counts[i % 3] = (a if "a" in who else 0, d if "d" in who else 0)
            return table

        T_USES = {l: t_uses(l) for l in (1, 2, 3)}

        def segments(layer, j):
            if j == 0:
                return [(0, 0, P)], [(0, 0)]
            if layer == 3:
                b = band_tiles(j)
                return ([(0, CACHE_TILE * P, P), (P, b[0] * P, len(b) * P)],
                        [(P + i * P, kt) for i, kt in enumerate(b)] + [(0, CACHE_TILE)])
            half = (NT * P) // 2
            return ([(0, P, half), (BANK, P + half, half)], [(i * P, 1 + i) for i in range(NT)])

        def score_view(ps, layer, j):
            if j == 0:
                return ps[:, 0, 0:P], lambda b: b[:, 0:P]
            if layer == 3:
                n = (1 + len(band_tiles(j))) * P
                return ps[:, 0, 0:n], lambda b: b[:, 0:n]
            half = (NT * P) // 2
            return ps[:, :, 0:half], lambda b: b[:, :].rearrange("p (a n) -> p a n", a=2)

        def runs(tiles):
            out = []
            for kt in sorted(tiles):
                if out and out[-1][-1] == kt - 1:
                    out[-1].append(kt)
                else:
                    out.append([kt])
            return [(r[0], len(r)) for r in out]

        def tbank(l, key):
            return psB[:, T_USES[l][key][0] % 3, :]

        OUT_LAT = psB[:, 3, :]

        CACHE_LOADS, n = {1: [], 2: [], 3: []}, [0, 0]
        for l in (1, 2, 3):
            for h in range(DIFF_HEADS if l == 2 else KV_HEADS):
                n[h % 2] += 32
                CACHE_LOADS[l].append(n[h % 2])
        ATT_DONE = {1: KT, 2: 1, 3: KT}
        NORMED = {0: []}
        for l in (1, 2, 3):
            heads = 4 * [8] if l == 2 else [8, 8, KV_HEADS]
            NORMED[l] = [(c, j, n) for c, n in enumerate(heads) for j in range(NT)]

        def probs_parts(l, h, j):
            tiles = [kt for _, kt in segments(l, j)[1]]
            out = []
            for i, (first, n) in enumerate(split(len(tiles))):
                rs_, o = [], 0
                for kt, k in runs(tiles[first:first + n]):
                    rs_.append((o, kt, k))
                    o += k * P
                out.append((("p", h, j, i), rs_))
            return out

        def t_before(eng, l, key):
            a, d = T_USES[l][key][3]
            if a:
                eng.wait_ge(s_ta[l], a)
            if d:
                eng.wait_ge(s_td[l], d)

        def transposes(pe, l, key, tiles):
            for i, (first, n) in enumerate(split(len(tiles))):
                t_before(pe, l, (*key, i))
                for x in range(n):
                    ins = pe.transpose(tbank(l, (*key, i))[:, x * P:(x + 1) * P], tiles[first + x], ident[:, :])
                ins.then_inc(s_t[l], 1)

        def transposes_twice(pe, l, key, tiles):
            for i, (first, n) in enumerate(split(len(tiles))):
                t_before(pe, l, (*key, i))
                bank = tbank(l, (*key, i))
                for x in range(n):
                    pe.transpose(bank[0:DH, x * P:(x + 1) * P], tiles[first + x], ident[:, :])
                for x in range(n):
                    ins = pe.matmul(bank[DH:P, x * P:(x + 1) * P], tiles[first + x], ident[:, :],
                                    start=True, stop=True)
                ins.then_inc(s_t[l], 1)

        def done_t(l, *key):
            return T_USES[l][key][0] + 1

        def taken_a(pe, l, *key):
            pe.wait_ge(s_ta[l], T_USES[l][key][1] + 1)

        def taken_d(eng, l, *key):
            eng.wait_ge(s_td[l], T_USES[l][key][2] + 1)

        def attention_pe(pe, l):
            kv = qkv[3]
            units = [(h, j) for h in range(HEADS) for j in range(NT)]

            def key_prep(g):
                c = D_MODEL + g * DH
                pe.wait_ge(s_cache[g % 2], CACHE_LOADS[l][g])
                transposes_twice(pe, l, ("k", g), [kv[:, i, c:c + DH] for i in range(NT)] + [k_cache[g % 2][:, :]])

            def query_prep(h):
                transposes_twice(pe, l, ("q", h), [kv[:, i, h * DH:(h + 1) * DH] for i in range(NT)])

            def scores(u):
                h, j = units[u]
                if j == 0:
                    g = h // GROUP
                    taken_d(pe, l, "q", h, 1)
                    if h % GROUP == 0:
                        taken_d(pe, l, "k", g, 1)
                if u >= 2:
                    pe.wait_ge(s_e[l], u - 1)
                ps = psA[:, 2 * (u % 2):2 * (u % 2) + 2, :].rearrange("p a n -> p (a n)")
                q = query[h % 2][:, j * P:(j + 1) * P]
                segs, _ = segments(l, j)
                b = band_tiles(j) if l == 3 and j else []
                masks = [(P + (kt - b[0]) * P, m) for m, kt in ((0, j - 1), (1, j + 1)) if kt in b]
                shared = l == 3 and j > 0
                for i, (o, c, n) in enumerate(segs):
                    pe.matmul(ps[:, o:o + n], q, key_hi[h // GROUP % 2][:, c:c + n], start=not (shared and i), stop=False,
                              skip_group_check=shared)
                for i, (o, c, n) in enumerate(segs):
                    ins = pe.matmul(ps[:, o:o + n], q, key_lo[h // GROUP % 2][:, c:c + n], start=False,
                                    stop=not shared or (i == 1 and not masks), skip_group_check=shared)
                for i, (o, m) in enumerate(masks):
                    ins = pe.matmul(ps[:, o:o + P], ident_r[:, :], mask_r[:, m, :], start=False,
                                    stop=(i == len(masks) - 1), skip_group_check=True)
                ins.then_inc(s_s[l], 1)

            def probs_t(u):
                h, j = units[u]
                pe.wait_ge(s_p[l], u + 1)
                _, tiles = segments(l, j)
                transposes(pe, l, ("p", h, j), [probs[u % 2][:, c:c + P] for c, _ in tiles])

            def pv(h):
                g, odd = h // GROUP, h % 2
                pe.wait_ge(s_vlo[l], g + 1)
                taken_d(pe, l, "p", h, NT - 1, len(split(n_keys(l, NT - 1) // P)) - 1)
                if h >= 2 and not odd:
                    pe.wait_ge(s_att[l], h // 2)

                def passes(o, kt, hi, lo, side, first, last):
                    a = (DH, 0)[side]
                    vh, vl = v_hi[:, kt, a:a + P], v_lo[:, kt, a:a + P]
                    pe.matmul(o, vh, hi, start=first, stop=False, skip_group_check=True)
                    pe.matmul(o, vh, lo, start=False, stop=False, skip_group_check=True)
                    return pe.matmul(o, vl, hi, start=False, stop=last, skip_group_check=True)

                if odd:
                    t_before(pe, l, ("c", h, 0))
                    out = tbank(l, ("c", h, 0))[:, 0:P]
                    for i, x in enumerate((h - 1, h)):
                        ins = passes(out, 0, ptc[x % 4][:, 0, :], ptc[x % 4][:, 1, :], i, i == 0, i == 1)
                    ins.then_inc(s_t[l], 1)
                order = [CACHE_TILE] + list(range(1, NT))
                for i, kt in enumerate(order):
                    qs = [j for j in range(1, NT) if kt == CACHE_TILE or l == 1 or kt in band_tiles(j)]
                    x, y = (qs[0] - 1) * P, qs[-1] * P
                    ins = passes(OUT_LAT[:, x:y], kt, pt_hi[odd][:, kt - 1, x:y], pt_lo[odd][:, kt - 1, x:y],
                                 odd, i == 0 and not odd, i == NT - 1 and odd == 1)
                ins.then_inc(s_pv[l], 1)

            pe.wait_ge(s_qkv, l)
            key_prep(0)
            query_prep(0)
            scores(0)
            for u in range(len(units) + 1):
                h, j = units[u] if u < len(units) else (HEADS, 0)
                if u + 1 < len(units):
                    scores(u + 1)
                if u:
                    probs_t(u - 1)
                if j == 1 and h % GROUP == GROUP - 1 and h + 1 < HEADS:
                    key_prep(h // GROUP + 1)
                if j == 2:
                    if h:
                        pv(h - 1)
                    if h + 1 < HEADS:
                        query_prep(h + 1)
            pv(HEADS - 1)

        def attention_diff_pe(pe, l):
            kv = qkv[6]
            units = [(h, j) for h in range(DIFF_HEADS) for j in range(NT)]

            def prep(h, m):
                c = h * P + m * DH
                if m == 0:
                    pe.wait_ge(s_cache[h % 2], CACHE_LOADS[l][h])
                transposes_twice(pe, l, ("k", h, m), [kv[:, i, D_MODEL + c:D_MODEL + c + DH] for i in range(NT)]
                                 + [k_cache_d[h % 2][:, m * DH:(m + 1) * DH]])
                transposes_twice(pe, l, ("q", h, m), [kv[:, i, c:c + DH] for i in range(NT)])

            def scores(u, m):
                h, j = units[u]
                segs, _ = segments(l, j)
                if j == 0:
                    taken_d(pe, l, "q", h, m, 1)
                if u >= 1:
                    pe.wait_ge(s_e[l], 2 * (u - 1) + m + 1)
                ps = psA[:, 2 * m:2 * m + 2, :].rearrange("p a n -> p (a n)")
                q = queryd[h % 2][m][:, j * P:(j + 1) * P]
                kh, kl = keyd_hi[(2 * h + m) % 3], keyd_lo[(2 * h + m) % 3]
                for o, c, n in segs:
                    pe.matmul(ps[:, o:o + n], q, kh[:, c:c + n], start=True, stop=False)
                    ins = pe.matmul(ps[:, o:o + n], q, kl[:, c:c + n], start=False, stop=True)
                ins.then_inc(s_s[l], 1)

            def probs_t(u):
                h, j = units[u]
                pe.wait_ge(s_p[l], u + 1)
                _, tiles = segments(l, j)
                transposes(pe, l, ("p", h, j), [probs_d[u % 2][0][:, c:c + P] for c, _ in tiles])

            def pv(u):
                h, j = units[u]
                taken_d(pe, l, "p", h, j, 1 if j else 0)
                if j == 0:
                    pe.wait_ge(s_vlo[l], h + 1)
                    t_before(pe, l, ("c", h, 0))
                elif j == 1 and h:
                    pe.wait_ge(s_osqa, h)
                o = tbank(l, ("c", h, 0))[:, 0:P] if j == 0 else OUT_LAT[:, (j - 1) * P:j * P]
                _, tiles = segments(l, j)
                for i, (_, kt) in enumerate(tiles):
                    hi, lo = ptd_hi[u % 2][:, i, :], ptd_lo[u % 2][:, i, :]
                    pe.matmul(o, lo, vd_hi[h % 2][:, kt, :], start=(i == 0), stop=False)
                    pe.matmul(o, hi, vd_hi[h % 2][:, kt, :], start=False, stop=False)
                    ins = pe.matmul(o, hi, vd_lo[h % 2][:, kt, :], start=False, stop=(i == len(tiles) - 1))
                ins.then_inc(s_t[l] if j == 0 else s_pv[l], 1)

            def out_t(h):
                pe.wait_ge(s_on, h + 1)
                for part, tiles in enumerate(([out_c[h % 2][:, :]], [out_d[:, i, :] for i in range(1, NT)])):
                    key = ("o", h, part)
                    t_before(pe, l, key)
                    for i, src in enumerate(tiles):
                        ins = pe.transpose(tbank(l, key)[:, i * P:(i + 1) * P], src, ident[:, :])
                    ins.then_inc(s_t[l], 1)

            pe.wait_ge(s_qkv, l)
            prep(0, 0)
            prep(0, 1)
            scores(0, 0)
            scores(0, 1)
            for u in range(len(units) + 3):
                h, j = units[u] if u < len(units) else (DIFF_HEADS, u - len(units))
                more = u + 1 < len(units)
                if more:
                    scores(u + 1, 0)
                if u >= 3:
                    pv(u - 3)
                if more:
                    scores(u + 1, 1)
                if 1 <= u <= len(units):
                    probs_t(u - 1)
                if j == 0 and h > 1:
                    out_t(h - 2)
                if j in (2, 3) and h + 1 < DIFF_HEADS:
                    prep(h + 1, j - 2)
            out_t(DIFF_HEADS - 1)

        def take_hi(act, l, dst, n, *key):
            for i, (first, k) in enumerate(split(n)):
                act.wait_ge(s_t[l], done_t(l, *key, i))
                act.activation(dst[:, first * P:(first + k) * P], tbank(l, (*key, i))[:, 0:k * P],
                               ACT.Copy).then_inc(s_ta[l], 1)

        def attention_act(act, own, l):
            kv = qkv[3]
            units = [(h, j) for h in range(HEADS) for j in range(NT)]
            loads = {"n": 0}

            def value_hi(g):
                act.wait_ge(s_cache[g % 2], CACHE_LOADS[l][g])
                if g:
                    act.wait_ge(s_pv[l], GROUP * g)
                c = D_MODEL + (KV_HEADS + g) * DH
                own(act.activation(v_hi[:, 0:NT, DH:2 * DH], kv[:, :, c:c + DH], ACT.Copy))
                act.activation(v_hi[:, NT, DH:2 * DH], v_cache[g % 2][:, :], ACT.Copy).then_inc(s_vhi[l], 1)

            def take_query(h):
                if h >= 2:
                    act.wait_ge(s_s[l], NT * (h - 1))
                take_hi(act, l, query[h % 2], NT, "q", h)

            def take_key(g):
                if g >= 2:
                    act.wait_ge(s_s[l], NT * GROUP * (g - 1))
                take_hi(act, l, key_hi[g % 2], KEY_TILES, "k", g)

            def exp(u):
                h, j = units[u]
                act.wait_ge(s_top[l], u + 1)
                if u >= 2:
                    p = units[u - 2]
                    act.wait_ge(s_t[l], done_t(l, "p", *p, len(split(n_keys(l, p[1]) // P)) - 1))
                src, shape = score_view(psA[:, 2 * (u % 2):2 * (u % 2) + 2, :], l, j)
                if l == 3:
                    own(act.activation(sink_e[u % 2][:, :], row[:, R_SINK + h:R_SINK + h + 1], ACT.Exp,
                                       bias=shift[u % 2][:, 0:1]))
                act.activation(shape(probs[u % 2]), src, ACT.Exp, bias=shift[u % 2][:, 0:1], scale=SCALE,
                               accum_out=total[u % 2][:, 0:1]).then_inc(s_e[l], 1)

            def take_probs(u):
                h, j = units[u]
                if j == 0:
                    if h >= 4:
                        act.wait_ge(s_pv[l], h - 2)
                    take_hi(act, l, ptc[h % 4][:, 0, :], 1, "p", h, j)
                    return
                if j == 1 and h >= 2:
                    act.wait_ge(s_pv[l], h - 1)
                for key, rs_ in probs_parts(l, h, j):
                    act.wait_ge(s_t[l], done_t(l, *key))
                    for i, (o, kt, n) in enumerate(rs_):
                        ins = act.activation(pt_hi[h % 2][:, kt - 1:kt - 1 + n, (j - 1) * P:j * P],
                                             tbank(l, key)[:, o:o + n * P].rearrange("p (a n) -> p a n", n=P),
                                             ACT.Copy)
                        if i < len(rs_) - 1:
                            own(ins)
                    ins.then_inc(s_ta[l], 1)

            def out_ctx_hi(h):
                d = h // 2
                take_hi(act, l, h_hi[:, d, CTX0:CTX0 + SEQ], 1, "c", h)

            def out_hi(h):
                act.wait_ge(s_pv[l], h + 1)
                act.activation(h_hi[:, h // 2, LAT0:LAT0 + DEC_SEQ], OUT_LAT, ACT.Copy).then_inc(s_ohi[l], 1)

            act.wait_ge(s_vzero, (1 if l == 1 else 2))
            take_key(0)
            take_query(0)
            value_hi(0)
            for u in range(len(units) + 1):
                h, j = units[u] if u < len(units) else (HEADS, 0)
                nk = h % GROUP == GROUP - 1 and h + 1 < HEADS
                if u < len(units):
                    exp(u)
                if u:
                    take_probs(u - 1)
                if j == 1 and nk:
                    take_key(h // GROUP + 1)
                if j == 2 and h and h % 2 == 0:
                    out_ctx_hi(h - 1)
                if j == 2 and h + 1 < HEADS:
                    take_query(h + 1)
                if j == 3:
                    if h and (h - 1) % 2:
                        out_hi(h - 1)
                    if h and h % GROUP == 0:
                        value_hi(h // GROUP)
            out_ctx_hi(HEADS - 1)
            out_hi(HEADS - 1)

        def attention_diff_act(act, own, l):
            kv = qkv[6]
            units = [(h, j) for h in range(DIFF_HEADS) for j in range(NT)]

            def prep(h, m):
                i = 2 * h + m
                if i >= 3:
                    act.wait_ge(s_s[l], 2 * NT * ((i - 3) // 2) + 2 * (NT - 1) + (i - 3) % 2 + 1)
                take_hi(act, l, keyd_hi[i % 3], KEY_TILES, "k", h, m)
                take_hi(act, l, queryd[h % 2][m], NT, "q", h, m)

            def value_hi(h):
                act.wait_ge(s_cache[h % 2], CACHE_LOADS[l][h])
                if h > 1:
                    act.wait_ge(s_pv[l], (NT - 1) * (h - 1))
                c = 2 * D_MODEL + h * P
                own(act.activation(vd_hi[h % 2][:, 0:NT, :], kv[:, :, c:c + P], ACT.Copy))
                act.activation(vd_hi[h % 2][:, NT, :], v_cache_d[h % 2][:, :], ACT.Copy).then_inc(s_vhi[l], 1)

            def exp(u):
                h, j = units[u]
                for m in range(2):
                    act.wait_ge(s_top[l], 2 * u + m + 1)
                    if u >= 2:
                        p = units[u - 2]
                        act.wait_ge(s_t[l], done_t(l, "p", *p, 1 if p[1] else 0))
                    src, shape = score_view(psA[:, 2 * m:2 * m + 2, :], l, j)
                    act.activation(shape(probs_d[u % 2][m]), src, ACT.Exp, bias=shift[u % 2][:, m:m + 1],
                                   scale=SCALE, accum_out=total[u % 2][:, m:m + 1]).then_inc(s_e[l], 1)

            def take_probs(u):
                h, j = units[u]
                if u >= 2:
                    x, y = units[u - 2]
                    if y:
                        act.wait_ge(s_pv[l], (NT - 1) * x + y)
                    else:
                        act.wait_ge(s_t[l], done_t(l, "c", x, 0))
                take_hi(act, l, ptd_hi[u % 2][:, :, :].rearrange("p a n -> p (a n)"), n_keys(l, j) // P, "p", h, j)

            def squares(o, h, j):
                return act.activation(o, o, ACT.Square, accum_out=out_sq[h % 2][:, j:j + 1])

            def out_ctx(h):
                o = tbank(l, ("c", h, 0))[:, 0:P]
                act.wait_ge(s_t[l], done_t(l, "c", h, 0))
                own(act.activation(out_c[h % 2][:, :], o, ACT.Copy))
                own.wait()
                squares(o, h, 0).then_inc(s_ta[l], 1)

            def out_copy(h):
                act.wait_ge(s_pv[l], (NT - 1) * (h + 1))
                if h:
                    act.wait_ge(s_t[l], done_t(l, "o", h - 1, 1))
                own(act.activation(out_d[:, 1:NT, :].rearrange("p a n -> p (a n)"), OUT_LAT, ACT.Copy))
                own.wait()
                for j in range(1, NT):
                    ins = squares(OUT_LAT[:, (j - 1) * P:j * P], h, j)
                    if j < NT - 1:
                        own(ins)
                ins.then_inc(s_osqa, 1)

            def out_hi(h):
                take_hi(act, l, h_hi[:, h, CTX0:CTX0 + SEQ], 1, "o", h)
                act.wait_ge(s_t[l], done_t(l, "o", h, 1))
                act.activation(h_hi[:, h, LAT0:LAT0 + DEC_SEQ], tbank(l, ("o", h, 1)), ACT.Copy).then_inc(s_ta[l], 1)

            act.wait_ge(s_lam, 1)
            act.activation(lam[:, 0:2], lam[:, 0:2], ACT.Exp).then_inc(s_lame, 1)
            prep(0, 0)
            prep(0, 1)
            value_hi(0)
            for u in range(len(units) + 4):
                h, j = units[u] if u < len(units) else (DIFF_HEADS, u - len(units))
                if j == 3 and h:
                    out_copy(h - 1)
                if u < len(units):
                    exp(u)
                if j == 3 and u - 3 < len(units):
                    out_ctx(h)
                if 1 <= u <= len(units):
                    take_probs(u - 1)
                if h < DIFF_HEADS:
                    if j == 0 and h:
                        value_hi(h)
                if j == 0 and h > 1:
                    out_hi(h - 2)
                if j in (2, 3) and h + 1 < DIFF_HEADS:
                    prep(h + 1, j - 2)
            out_hi(DIFF_HEADS - 1)

        def pool_dve(dve, own, md, add_out, mod_copy, mod_first_bias):
            for b in hp:
                own(dve.memset(b[:, :], 0.0))
            own.wait()
            dve.wait_ge(s_count, 16)
            spans = ((CTX0, SEQ, PAD, 0), (LAT0, DEC_SEQ, 2 * PAD + SEQ, SEQ))

            def pooled(d):
                g = d // 2
                dve.wait_ge(s_h, d + 1)
                if d:
                    dve.wait_ge(s_pooled, d)
                for c, w, o, _ in spans:
                    own(dve.tensor_tensor(hp[0][:, o:o + w], h_hi[:, d, c:c + w].bitcast(F32),
                                          h_lo[:, d, c:c + w].bitcast(F32), ALU.add))
                own.wait()
                src, a, b = 0, 1, 0
                n = PC - 16
                for step in range(g + 1):
                    dst = 1 if src != 1 else 2
                    own(dve.tensor_tensor(hp[dst][:, 8:8 + n], hp[src][:, 8 - a:8 - a + n],
                                          hp[src][:, 8 + b:8 + b + n], ALU.add))
                    own.wait()
                    src = dst
                    a, b = (1, 1) if step == 0 else (2 * a, 2 * b)
                for c, w, o, i in spans:
                    own(dve.tensor_tensor(hp[src][:, o:o + w], hp[src][:, o:o + w], inv_count[:, g, i:i + w], ALU.mult))
                own.wait()
                for k, (c, w, o, _) in enumerate(spans):
                    ins = dve.tensor_tensor(hp[2][:, o:o + w], hp[src][:, o:o + w], hp[0][:, o:o + w], ALU.subtract)
                    if k == 0:
                        own(ins)
                ins.then_inc(s_pool32, 1)
                dve.wait_ge(s_pooled_hi, d + 1)
                for k, (c, w, o, _) in enumerate(spans):
                    ins = dve.tensor_tensor(h_lo[:, d, c:c + w], hp[2][:, o:o + w],
                                            h_hi[:, d, c:c + w].bitcast(F32), ALU.subtract)
                    if k == 0:
                        own(ins)
                ins.then_inc(s_pooled, 1)

            for g in range(5):
                for d in (2 * g, 2 * g + 1):
                    if d < KT:
                        mod_copy(FIRST_PASSES + d)
                        pooled(d)
                        mod_first_bias(FIRST_PASSES + d)
                if g == 0:
                    dve.wait_ge(s_modok, FIRST_PASSES + 2)
                    own(dve.tensor_tensor(pool_gate[:, :, :], md[:, MOD_G1:MOD_G1 + KT, :],
                                          vec[:, V_POOL:V_POOL + KT].unsqueeze(2).to_broadcast([P, KT, 2]), ALU.mult))
                    own.wait()
                if g:
                    dve.wait_ge(s_mx[0], g)
                    add_out(0, 2 * g - 2, pool_gate, s_mxadd[0])
                    dve.wait_ge(s_wused, 2 * g)
                    add_out(1, 2 * g - 1, pool_gate, s_mxadd[0])

        def qkv_dve(dve, own, lo_w, l):
            nq = QKV_CHUNKS[l]
            kv = qkv[nq]
            c0 = FIRST_CHUNK[l]
            dve.wait_ge(s_rope, 16 * l)
            dve.wait_ge(s_small, 48)
            for i, r in ((0, R_QN), (1, R_KN)):
                g = row[:, r + (l - 1) * DH:r + l * DH]
                own(dve.tensor_tensor(rope_cos[:, i, :, :], rope_raw[:, 0, :, :],
                                      g.unsqueeze(1).to_broadcast([P, NT - 1, DH]), ALU.mult))
                for ax in range(2):
                    for hf in range(2):
                        a = ax * 32 + hf * 16
                        b = ax * 32 + (1 - hf) * 16
                        own(dve.tensor_tensor(rope_sin[:, i, :, a:a + 16], rope_raw[:, 1, :, a:a + 16],
                                              g[:, b:b + 16].unsqueeze(1).to_broadcast([P, NT - 1, 16]), ALU.mult))
            if l == 3:
                dve.wait_ge(s_mask, 16)
                own(dve.tensor_copy(mask_r[:, :, :], mask_raw[:, :, :]))
                own(dve.tensor_copy(ident_r[:, :], ident[:, :]))
            own.wait()

            def means(i):
                c, j, n = NORMED[l][i]
                dve.wait_ge(s_qe[l], c * NT + j + 1)
                own(dve.tensor_reduce(qms[i % 2][:, 0:n],
                                      qkv_sq[i % 2][:, 0:n * DH].rearrange("p (h n) -> p h n", n=DH), AX_X, ALU.add))
                own.wait()
                dve.tensor_scalar(qms[i % 2][:, 0:n], qms[i % 2][:, 0:n], 1.0 / DH, EPS, ALU.mult,
                                  ALU.add).then_inc(s_qms[l], 1)

            def rotate(i):
                c, j, n = NORMED[l][i]
                is_key = c >= 2
                x = kv[:, j, c * UNIT:c * UNIT + n * DH]
                xh = x.rearrange("p (h n) -> p h n", n=DH)
                dve.wait_ge(s_qrs[l], i + 1)
                own(dve.tensor_tensor(xh, xh, qrs[i % 2][:, 0:n].unsqueeze(2).to_broadcast([P, n, DH]), ALU.mult))
                own.wait()
                if j == 0:
                    g = row[:, (R_KN if is_key else R_QN) + (l - 1) * DH:][:, 0:DH]
                    own(dve.tensor_tensor(xh, xh, g.unsqueeze(1).to_broadcast([P, n, DH]), ALU.mult))
                    return
                ra, rb = rope_a[:, 0:n * DH], rope_b[:, 0:n * DH]
                own(dve.tensor_tensor(ra.rearrange("p (h n) -> p h n", n=DH), xh,
                                      rope_cos[:, int(is_key), j - 1, :].unsqueeze(1).to_broadcast([P, n, DH]),
                                      ALU.mult))
                for hf in range(2):
                    def part(b, f):
                        return b.rearrange("p (h a f n) -> p h a f n", a=2, f=2, n=16)[:, :, :, f, :]
                    sn = rope_sin[:, int(is_key), j - 1, :].rearrange("p (a f n) -> p a f n", a=2, f=2)[:, :, hf, :]
                    own(dve.tensor_tensor(part(rb, hf), part(x, 1 - hf),
                                          sn.unsqueeze(1).to_broadcast([P, n, 2, 16]), ALU.mult))
                own.wait()
                own(dve.tensor_tensor(x, ra, rb, ALU.add))

            index = {(c, j): i for i, (c, j, _) in enumerate(NORMED[l])}
            done = 0
            for c in range(nq):
                for j in range(NT):
                    if j == NT - 1 and c < nq - 1:
                        for u in range(UNITS):
                            lo_w(u, UNITS * (c0 + c + 1) + u + 1)
                    i = index.get((c, j))
                    if i is not None:
                        means(i)
                        if i:
                            rotate(i - 1)
                        done = i
            rotate(done)
            own.wait()
            dve.wait_ge(s_qe[l], nq * NT)
            dve.tensor_copy(mark[:, l:l + 1], ones2[:, 0:1]).then_inc(s_qkv, 1)

        def softmax_small(dve, own, l, i, m, h, u):
            if l == 3:
                return dve.tensor_scalar(shift[i][:, m:m + 1], top[i][:, m:m + 1], -SCALE, nsink[:, h:h + 1],
                                         ALU.mult, ALU.min)
            return dve.tensor_scalar(shift[i][:, m:m + 1], top[i][:, m:m + 1], -SCALE, None, ALU.mult)

        def lo_part(dve, out, src, hi):
            return dve.tensor_tensor(out, src, hi.bitcast(F32), ALU.subtract)

        def take_lo(dve, l, dst, hi, n, *key):
            for i, (first, k) in enumerate(split(n)):
                taken_a(dve, l, *key, i)
                c = slice(first * P, (first + k) * P)
                lo_part(dve, dst[:, c], tbank(l, (*key, i))[:, 0:k * P], hi[:, c]).then_inc(s_td[l], 1)

        def take_query_lo(dve, l, q, *key):
            for i, (first, k) in enumerate(split(NT)):
                taken_a(dve, l, *key, i)
                x = q[DH:P, first * P:(first + k) * P]
                lo_part(dve, x, tbank(l, (*key, i))[DH:P, 0:k * P], x).then_inc(s_td[l], 1)

        def attention_dve(dve, own, l):
            kv = qkv[3]
            units = [(h, j) for h in range(HEADS) for j in range(NT)]
            for b in (v_hi, v_lo):
                own(dve.memset(b[:, :, :].bitcast(mybir.dt.uint32), 0))
            own.wait()
            if l == 3:
                own(dve.tensor_scalar(nsink[:, :], row[:, R_SINK:R_SINK + HEADS], -1.0, None, ALU.mult))
            dve.tensor_copy(mark[:, l + 4:l + 5], ones2[:, 0:1]).then_inc(s_vzero, 1)

            def value_lo(g):
                dve.wait_ge(s_vhi[l], g + 1)
                c = D_MODEL + (KV_HEADS + g) * DH
                own(lo_part(dve, v_lo[:, 0:NT, DH:2 * DH], kv[:, :, c:c + DH], v_hi[:, 0:NT, DH:2 * DH]))
                lo_part(dve, v_lo[:, NT, DH:2 * DH], v_cache[g % 2][:, :], v_hi[:, NT, DH:2 * DH]).then_inc(s_vlo[l], 1)

            def take_key(g):
                take_lo(dve, l, key_lo[g % 2], key_hi[g % 2], KEY_TILES, "k", g)

            def softmax(u):
                if u < len(units):
                    dve.wait_ge(s_s[l], u + 1)
                    src, _ = score_view(psA[:, 2 * (u % 2):2 * (u % 2) + 2, :], l, units[u][1])
                    own(dve.tensor_reduce(top[u % 2][:, 0:1], src,
                                          mybir.AxisListType.XY if len(src.shape) == 3 else AX_X, ALU.max))
                i = (u - 1) % 2
                if 1 <= u <= len(units):
                    dve.wait_ge(s_e[l], u)
                    if l == 3:
                        own(dve.tensor_tensor(total[i][:, 0:1], total[i][:, 0:1], sink_e[i][:, :], ALU.add))
                        own.wait()
                    own(dve.reciprocal(norm[i][:, 0:1], total[i][:, 0:1]))
                own.wait()
                if u < len(units):
                    softmax_small(dve, own, l, u % 2, 0, units[u][0], u).then_inc(s_top[l], 1)
                if 1 <= u <= len(units):
                    n = n_keys(l, units[u - 1][1])
                    dve.tensor_scalar(probs[i][:, 0:n], probs[i][:, 0:n], norm[i][:, 0:1], None,
                                      ALU.mult).then_inc(s_p[l], 1)

            def take_probs(u):
                h, j = units[u]
                if j == 0:
                    take_lo(dve, l, ptc[h % 4][:, 1, :], ptc[h % 4][:, 0, :], 1, "p", h, j)
                    return
                for key, rs_ in probs_parts(l, h, j):
                    taken_a(dve, l, *key)
                    for i, (o, kt, n) in enumerate(rs_):
                        ins = lo_part(dve, pt_lo[h % 2][:, kt - 1:kt - 1 + n, (j - 1) * P:j * P],
                                      tbank(l, key)[:, o:o + n * P].rearrange("p (a n) -> p a n", n=P),
                                      pt_hi[h % 2][:, kt - 1:kt - 1 + n, (j - 1) * P:j * P])
                        if i < len(rs_) - 1:
                            own(ins)
                    ins.then_inc(s_td[l], 1)

            def out_ctx_lo(h):
                d = h // 2
                take_lo(dve, l, h_lo[:, d, CTX0:CTX0 + SEQ], h_hi[:, d, CTX0:CTX0 + SEQ], 1, "c", h)

            def out_lo(h):
                d = h // 2
                dve.wait_ge(s_ohi[l], d + 1)
                ins = lo_part(dve, h_lo[:, d, LAT0:LAT0 + DEC_SEQ], OUT_LAT, h_hi[:, d, LAT0:LAT0 + DEC_SEQ])
                ins.then_inc(s_att[l], 1)

            take_key(0)
            take_query_lo(dve, l, query[0], "q", 0)
            value_lo(0)
            for u in range(len(units) + 2):
                h, j = units[u] if u < len(units) else (HEADS, u - len(units))
                softmax(u)
                if u >= 2:
                    take_probs(u - 2)
                if j == 2 and h % GROUP == GROUP - 1 and h + 1 < HEADS:
                    take_key(h // GROUP + 1)
                if j == 3:
                    if h and (h - 1) % 2:
                        out_ctx_lo(h - 1)
                    if h + 1 < HEADS:
                        take_query_lo(dve, l, query[(h + 1) % 2], "q", h + 1)
                    if h and (h - 1) % 2:
                        out_lo(h - 1)
                    if h and h % GROUP == 0:
                        value_lo(h // GROUP)
            out_ctx_lo(HEADS - 1)
            out_lo(HEADS - 1)

        def attention_diff_dve(dve, own, l):
            kv = qkv[6]
            units = [(h, j) for h in range(DIFF_HEADS) for j in range(NT)]
            for i in range(2):
                r = R_LAM + 2 * i * DH
                own(dve.tensor_tensor(lam_tmp[:, :], row[:, r:r + DH], row[:, r + DH:r + 2 * DH], ALU.mult))
                own.wait()
                ins = dve.tensor_reduce(lam[:, i:i + 1], lam_tmp[:, :], AX_X, ALU.add)
                if i == 0:
                    own(ins)
                    own.wait()
            ins.then_inc(s_lam, 1)
            dve.wait_ge(s_lame, 1)
            own(dve.tensor_tensor(lam[:, 2:3], lam[:, 1:2], lam[:, 0:1], ALU.subtract))
            own.wait()
            own(dve.tensor_scalar(lam[:, 3:4], lam[:, 2:3], lam_init(l), None, ALU.subtract))
            own(dve.tensor_scalar(sub_g[:, :], row[:, R_SUB:R_SUB + P], 1.0 - lam_init(l), None, ALU.mult))
            own.wait()

            def value_lo(h):
                dve.wait_ge(s_vhi[l], h + 1)
                c = 2 * D_MODEL + h * P
                own(lo_part(dve, vd_lo[h % 2][:, 0:NT, :], kv[:, :, c:c + P], vd_hi[h % 2][:, 0:NT, :]))
                lo_part(dve, vd_lo[h % 2][:, NT, :], v_cache_d[h % 2][:, :],
                        vd_hi[h % 2][:, NT, :]).then_inc(s_vlo[l], 1)

            def prep(h, m):
                i = (2 * h + m) % 3
                take_lo(dve, l, keyd_lo[i], keyd_hi[i], KEY_TILES, "k", h, m)
                take_query_lo(dve, l, queryd[h % 2][m], "q", h, m)

            def maximum(u, m):
                h, j = units[u]
                dve.wait_ge(s_s[l], 2 * u + m + 1)
                src, _ = score_view(psA[:, 2 * m:2 * m + 2, :], l, j)
                own(dve.tensor_reduce(top[u % 2][:, m:m + 1], src,
                                      mybir.AxisListType.XY if len(src.shape) == 3 else AX_X, ALU.max))
                own.wait()
                softmax_small(dve, own, l, u % 2, m, h, u).then_inc(s_top[l], 1)

            def combine(u):
                h, j = units[u]
                i, n = u % 2, n_keys(l, j)
                a, b = (x[:, 0:n] for x in probs_d[i])
                dve.wait_ge(s_e[l], 2 * u + 2)
                own(dve.reciprocal(norm[i][:, :], total[i][:, :]))
                own.wait()
                own(dve.tensor_scalar(norm[i][:, 1:2], norm[i][:, 1:2], lam[:, 3:4], None, ALU.mult))
                own(dve.tensor_scalar(a, a, norm[i][:, 0:1], None, ALU.mult))
                own.wait()
                dve.scalar_tensor_tensor(out=a, in0=b, scalar=norm[i][:, 1:2], in1=a, op0=ALU.mult,
                                         op1=ALU.add).then_inc(s_p[l], 1)

            def take_probs(u):
                h, j = units[u]
                lo, hi = (b[u % 2][:, :, :].rearrange("p a n -> p (a n)") for b in (ptd_lo, ptd_hi))
                take_lo(dve, l, lo, hi, n_keys(l, j) // P, "p", h, j)

            def out_means(h):
                dve.wait_ge(s_osqa, h + 1)
                dve.tensor_scalar(ms[:, :], out_sq[h % 2][:, :], 1.0 / P, EPS, ALU.mult, ALU.add).then_inc(s_oms, 1)

            def out_norm(h):
                dve.wait_ge(s_ors, h + 1)
                for j in range(NT):
                    o = out_c[h % 2][:, :] if j == 0 else out_d[:, j, :]
                    ins = dve.scalar_tensor_tensor(out=o, in0=o, scalar=rs[:, j:j + 1],
                                                   in1=sub_g[:, :], op0=ALU.mult, op1=ALU.mult)
                    if j < NT - 1:
                        own(ins)
                ins.then_inc(s_on, 1)

            def out_lo(h):
                take_lo(dve, l, h_lo[:, h, CTX0:CTX0 + SEQ], h_hi[:, h, CTX0:CTX0 + SEQ], 1, "o", h)
                taken_a(dve, l, "o", h, 1)
                lo_part(dve, h_lo[:, h, LAT0:LAT0 + DEC_SEQ], tbank(l, ("o", h, 1)),
                        h_hi[:, h, LAT0:LAT0 + DEC_SEQ]).then_inc(s_td[l], 1)

            prep(0, 0)
            prep(0, 1)
            value_lo(0)
            for u in range(len(units) + 4):
                h, j = units[u] if u < len(units) else (DIFF_HEADS, u - len(units))
                if u < len(units):
                    maximum(u, 0)
                    maximum(u, 1)
                if 1 <= u <= len(units):
                    combine(u - 1)
                if 2 <= u < len(units) + 2:
                    take_probs(u - 2)
                if j == 1 and h > 1:
                    out_lo(h - 2)
                if h < DIFF_HEADS:
                    if j == 0 and h:
                        value_lo(h)
                    if j in (3, 4) and h + 1 < DIFF_HEADS:
                        prep(h + 1, j - 3)
                if j == 3 and h:
                    out_means(h - 1)
                    out_norm(h - 1)
            out_lo(DIFF_HEADS - 1)
            taken_d(dve, l, "o", DIFF_HEADS - 1, 1)
            dve.tensor_copy(mark[:, 0:1], ones2[:, 0:1]).then_inc(s_att[l], 1)

        @block.sync
        def _(sp):
            def load_w(c, half, late=0):
                if isinstance(c, int) and c >= N_CHUNKS:
                    return
                if not isinstance(c, int) or c >= 1:
                    sp.wait_ge(s_wlo, UNITS * (c - 1) + UNITS // 2 * (half + 1))
                n = UNITS // 2
                sp.dma_start(w_stage[:, half * n:(half + 1) * n, :],
                             t["weights"][ds(c, 1), :, half * n * UNIT:(half + 1) * n * UNIT]
                             .rearrange("a p n -> (a p) n")).then_inc(s_w[half], 16)

            def load_wo(q):
                sp.dma_start(wo_stage[:, :, :],
                             t["w_out"][ds(q, 1), :, :].rearrange("a p n -> (a p) n")).then_inc(s_wo, 16)

            def load_m(mp, pair):
                for g in range(2):
                    sp.dma_start(m_stage[pair][:, g, :, :],
                                 t["w_mod"][ds(mp, 1), :, g, :].rearrange("a p n -> (a p) n")
                                 ).then_inc(s_m[pair][g], 16)

            sp.dma_start(vec[:, :], t["vec"]).then_inc(s_small, 16)
            sp.dma_start(ident[:, :], t["ident"]).then_inc(s_small, 16)
            load_m(0, 0)
            load_m(1, 1)
            sp.dma_start(xT[:, :, :].rearrange("p a n -> p (a n)"), t["xT"]).then_inc(s_x, 16)
            for m in range(2, 6):
                sp.wait_ge(s_mraw, 2 * (m - 1))
                load_m(m, m % 2)
            load_w(0, 0)
            load_w(0, 1)
            sp.dma_start(inv_count[:, :, :].rearrange("p a n -> p (a n)"), t["inv_count"]).then_inc(s_count, 16)
            sp.dma_start(row[:, :], t["row"]).then_inc(s_small, 16)
            for m in range(6, MOD_PASSES):
                sp.wait_ge(s_mraw, 2 * (m - 1))
                load_m(m, m % 2)
            load_w(1, 0)
            load_w(1, 1)

            for l in range(DEPTH):
                c0 = FIRST_CHUNK[l]
                if l == 0:
                    load_w(c0 + 2, 0)
                    load_w(c0 + 2, 1)
                    sp.wait_ge(s_mxadd[0], KT)
                    load_wo(0)
                else:
                    nq = QKV_CHUNKS[l]
                    kv = qkv[nq]
                    sp.wait_ge(s_o[l - 1], KT * ITERS)
                    sp.dma_start(rope_raw[:, :, :, :].rearrange("p a b n -> p (a b n)"),
                                 t["rope"]).then_inc(s_rope, 16)
                    if l == 3:
                        sp.dma_start(mask_raw[:, :, :].rearrange("p a n -> p (a n)"), t["mask"]).then_inc(s_mask, 16)
                    for c in range(nq - 1):
                        load_w(c0 + c + 2, 0)
                        if l != 2 or c < nq - 2:
                            load_w(c0 + c + 2, 1)
                    sp.wait_ge(s_qkv, l)
                    kw = D_MODEL if l == 2 else KV_HEADS * DH
                    for i, name in enumerate(("k", "v")):
                        sp.dma_start(t[f"{name}{l}"], kv[:, 0, D_MODEL + i * kw:D_MODEL + (i + 1) * kw]
                                     ).then_inc(s_kv_out, 16)
                    heads = DIFF_HEADS if l == 2 else KV_HEADS
                    n = P if l == 2 else DH
                    for h in range(heads):
                        if h >= 2:
                            sp.wait_ge(s_t[l], done_t(l, "k", h - 2, *((1,) if l == 2 else ()), 1))
                            sp.wait_ge(s_vlo[l], h - 1)
                        kc, vc = (k_cache_d, v_cache_d) if l == 2 else (k_cache, v_cache)
                        sp.dma_start(kc[h % 2][:, :], t[f"ck{l}"][:, h * n:(h + 1) * n]).then_inc(s_cache[h % 2], 16)
                        sp.dma_start(vc[h % 2][:, :], t[f"cv{l}"][:, h * n:(h + 1) * n]).then_inc(s_cache[h % 2], 16)
                    sp.wait_ge(s_att[l], ATT_DONE[l])
                    if l == 2:
                        load_w(c0 + nq, 1)
                    sp.wait_ge(s_kv_out, 32 * l)
                    load_wo(ITERS * l)
                    if l < DEPTH - 1:
                        load_m(MOD_PASSES * (l + 1), 0)
                    for c in (nq - 1, nq, nq + 1):
                        load_w(c0 + c + 2, 0)
                        load_w(c0 + c + 2, 1)
                if l == 0:
                    sp.wait_ge(s_mraw, 2 * MOD_PASSES)
                    load_m(MOD_PASSES, 0)
                cf = FFN_CHUNK[l]

                def ffn_loads(it, last):
                    load_w(it + (cf + 2), 0)
                    if not last:
                        sp.wait_ge(s_wolo, it * 2 + (2 * ITERS * l + 2))
                        load_wo(it + (ITERS * l + 1))
                    if l < DEPTH - 1:
                        sp.wait_ge(s_mraw, it * 2 + 2 * (MOD_PASSES * (l + 1) + 1))
                        load_m(it + (MOD_PASSES * (l + 1) + 1), 0)
                    load_w(it + (cf + 2), 1)

                ffn_loads(0, False)
                with sp.Fori(1, ITERS - 2) as it:
                    ffn_loads(it, False)
                ffn_loads(ITERS - 2, False)
                ffn_loads(ITERS - 1, True)
            for d in range(KT):
                sp.wait_ge(s_oadd[DEPTH - 1], KT * (ITERS - 1) + d + 1)
                sp.dma_start(t["yT"][:, d * COLS:(d + 1) * COLS], xT[:, d, :]).then_inc(s_y, 16)
            sp.wait_ge(s_y, 16 * KT)
            sp.wait_ge(s_kv_out, 32 * (DEPTH - 1))

        @block.gpsimd
        def _(pool):
            pool.memset(cond[:, :, :], 0.0).then_inc(s_pool, 1)
            pool.memset(minus_half[:, :], -0.5).then_inc(s_pool, 1)
            pool.wait_ge(s_pool, 2)

            def norm_pow(n):
                pool.wait_ge(s_ms, n + 1)
                pool.tensor_tensor(rs[:, :], ms[:, :], minus_half[:, 0:NT], ALU.pow).then_inc(s_rs, 1)

            for l in range(DEPTH):
                norm_pow(2 * l)
                for i in range(len(NORMED[l])):
                    n = NORMED[l][i][2]
                    pool.wait_ge(s_qms[l], i + 1)
                    pool.tensor_tensor(qrs[i % 2][:, 0:n], qms[i % 2][:, 0:n], minus_half[:, 0:n],
                                       ALU.pow).then_inc(s_qrs[l], 1)
                if l == 2:
                    for h in range(DIFF_HEADS):
                        pool.wait_ge(s_oms, h + 1)
                        pool.tensor_tensor(rs[:, :], ms[:, :], minus_half[:, 0:NT], ALU.pow).then_inc(s_ors, 1)
                norm_pow(2 * l + 1)

        @block.tensor
        def _(pe):
            def product(outs, w, x, first, last):
                for n, (wp, xp) in enumerate(((w[0], x[0]), (w[0], x[1]), (w[1], x[0]))):
                    for o, (a, b) in outs:
                        ins = pe.matmul(o, wp, xp[:, a:b], start=first and n == 0, stop=last and n == 2)
                return ins

            def halves(ps, slot):
                return [(ps[:, 2 * slot + i, 0:HALF], (i * HALF, (i + 1) * HALF)) for i in range(2)]

            def mod_half(pair, g, loads, outs):
                pe.wait_ge(s_m[pair][g], loads * 16)
                n = 2 * P // len(outs)
                for c, out in enumerate(outs):
                    for k in range(KT):
                        q = slice(32 * (k % 4), 32 * (k % 4 + 1))
                        ins = pe.matmul(out[q, :], cond[:, k, :], m_stage[pair][:, g, k, c * n:(c + 1) * n],
                                        start=(k < 4), stop=(k >= 4))
                ins.then_inc(s_mraw, 1)

            def mod_sum(rows, bank):
                pe.wait_ge(s_mrows, rows)
                for i in range(4):
                    ins = pe.matmul(bank[:, MOD_AT + 2 * i:MOD_AT + 2 * i + 2], mod_rows[:, i, :],
                                    vec[:, V_SUM:V_SUM + 2], start=True, stop=True)
                ins.then_inc(s_mod, 1)

            def mod_first(m):
                if m >= 2:
                    pe.wait_ge(s_mrows, m - 1)
                for g in range(2):
                    mod_half(m % 2, g, m // 2 + 1, [psA[:, m % 2, 2 * P * g:2 * P * (g + 1)]])

            def mod_first_sum(m):
                if m >= 2:
                    pe.wait_ge(s_modok, m - 1)
                mod_sum(m + 1, psA[:, 2 + m % 2, :])

            def mod_ffn(l, it, g):
                mod_half(0, g, it + (6 + MOD_PASSES * l + 1),
                         [psB[:, 2 * g + c, 3 * P:4 * P] for c in range(2)])

            def mod_ffn_sum(l, it):
                mod_sum(it * 2 + (MOD_PASSES * (2 * l + 1) + 2), psB[:, 3, :])

            def norm_pe(n):
                pe.wait_ge(s_sqsum, (KT - 1) * (n + 1))
                for j in range(NT):
                    c = tile_col(j)
                    ins = pe.matmul(psB[:, 0, 2 * j:2 * j + 2], sq_sum[:, c:c + P], ones2[:, :],
                                    start=True, stop=True)
                ins.then_inc(s_stat, 1)
                pe.wait_ge(s_rows, n + 1)
                for j in range(NT):
                    o = psB[:, 2, 0:P] if j == 0 else psB[:, 3, (j - 1) * P:j * P]
                    ins = pe.transpose(o, rstd_rows[:, j, :], ident[:, :])
                ins.then_inc(s_bc, 1)

            def proj_tiles(l, cg, dt, x):
                for k in range(KT):
                    if k % 4 == 0:
                        pe.wait_ge(s_wlo, UNITS * cg + 2 * (dt % 4) + k // 4 + 1)
                    u, c = 2 * (dt % 4) + k // 4, (k % 4) * P
                    ins = product(x[2], (w_hi[:, u, c:c + P], w_lo[:, u, c:c + P]),
                                  (x[0][:, k, :], x[1][:, k, :]), k == 0, k == KT - 1)
                    if k == 3:
                        ins.then_inc(s_wused, 1)
                ins.then_inc(s_wused, 1)

            pe.wait_ge(s_cond, 1)
            pe.wait_ge(s_small, 32)
            mod_first(0)
            for m in range(FIRST_PASSES):
                mod_first(m + 1)
                mod_first_sum(m)

            for l in range(DEPTH):
                norm_pe(2 * l)
                c0 = FIRST_CHUNK[l]
                if l == 0:
                    pe.wait_ge(s_const, 2)
                    mod_first(FIRST_PASSES + 1)
                    for g in range(4):
                        for m in range(FIRST_PASSES + 2 * g, FIRST_PASSES + 2 * g + 2):
                            mod_first_sum(m)
                            if m + 2 < MOD_PASSES:
                                mod_first(m + 2)
                        for c in range(2):
                            d = 2 * g + c
                            pe.wait_ge(s_pooled, 2 * g + 2)
                            if d >= 2:
                                pe.wait_ge(s_mxadd[0], d - 1)
                            for k in range(2):
                                pe.wait_ge(s_wlo, 2 * g + k + 1)
                                u = 2 * g + k
                                ins = product(halves(psB, d % 2),
                                              (w_hi[:, u, c * P:(c + 1) * P], w_lo[:, u, c * P:(c + 1) * P]),
                                              (h_hi[:, 2 * g + k, :], h_lo[:, 2 * g + k, :]), k == 0, k == 1)
                                if c == 1 and k == 0:
                                    ins.then_inc(s_wused, 1)
                            if c == 0:
                                ins.then_inc(s_mx[0], 1)
                            else:
                                ins.then_inc(s_wused, 1)
                else:
                    def qkv_step(i, k):
                        o, col = psA[:, i % 4, :], tile_col(i % NT)
                        hh, hl = h_hi[:, k, col:col + P], h_lo[:, k, col:col + P]
                        pe.matmul(o, hl, w_hi[:, k, :], start=(k == 0), stop=False)
                        pe.matmul(o, hh, w_hi[:, k, :], start=False, stop=False)
                        return pe.matmul(o, hh, w_lo[:, k, :], start=False, stop=(k == KT - 1))

                    for k in range(KT):
                        pe.wait_ge(s_wlo, UNITS * c0 + k + 1)
                        pe.wait_ge(s_h, KT * 2 * l + k + 1)
                        for i in range(4):
                            ins = qkv_step(i, k)
                            if k == KT - 1:
                                ins.then_inc(s_qp[l], 1)
                    for c in range(QKV_CHUNKS[l]):
                        for j in range(NT):
                            i = c * NT + j
                            if i < 4:
                                continue
                            pe.wait_ge(s_qe[l], i - 3)
                            for k in range(KT):
                                if j == 0:
                                    pe.wait_ge(s_wlo, UNITS * (c0 + c) + k + 1)
                                ins = qkv_step(i, k)
                                if j == NT - 1 and k < KT - 1:
                                    ins.then_inc(s_wused, 1)
                            if j < NT - 1:
                                ins.then_inc(s_qp[l], 1)
                            else:
                                ins.then_inc(s_wused, 1)
                    (attention_diff_pe if l == 2 else attention_pe)(pe, l)
                    pe.wait_ge(s_att[l], ATT_DONE[l])
                    for dt in range(KT):
                        if dt >= 2:
                            pe.wait_ge(s_mxadd[l], dt - 1)
                        proj_tiles(l, c0 + QKV_CHUNKS[l] + dt // 4, dt,
                                   (h_hi, h_lo, halves(psB, dt % 2)))

                norm_pe(2 * l + 1)
                cf = FFN_CHUNK[l]

                def u_tile(it, ft, first):
                    if not (first and ft < 2):
                        pe.wait_ge(s_u[l], it * 4 + (ft - 1))
                    proj_tiles(l, it + cf, ft, (h_hi, h_lo, halves(psA, ft % 2)))

                def first_u_tiles():
                    for k in range(KT):
                        if k % 4 == 0:
                            pe.wait_ge(s_wlo, UNITS * cf + k // 4 + 3)
                        pe.wait_ge(s_h, KT * (2 * l + 1) + k + 1)
                        for ft in range(2):
                            u, c = 2 * ft + k // 4, (k % 4) * P
                            ins = product(halves(psA, ft), (w_hi[:, u, c:c + P], w_lo[:, u, c:c + P]),
                                          (h_hi[:, k, :], h_lo[:, k, :]), k == 0, k == KT - 1)
                            if ft == 0 and k in (3, 7):
                                ins.then_inc(s_wused, 1)
                    ins.then_inc(s_wused, 2)

                def out_pass(it):
                    pe.wait_ge(s_g[l], it * 2 + 2)
                    pe.wait_ge(s_wolo, it * 2 + (2 * ITERS * l + 2))
                    for d in range(KT):
                        if d == 0 and l < DEPTH - 1:
                            pe.wait_ge(s_modok, it + (MOD_PASSES * (l + 1) + 1))
                        if not (isinstance(it, int) and it == 0 and d < 2):
                            pe.wait_ge(s_oadd[l], it * KT + (d - 1))
                        if d >= KT - 2 and l < DEPTH - 1:
                            mod_ffn(l, it + 1, d % 2)
                        for f in range(2):
                            ins = product(halves(psB, d % 2),
                                          (wo_hi[:, f, d * P:(d + 1) * P], wo_lo[:, f, d * P:(d + 1) * P]),
                                          (g_hi[:, f, :], g_lo[:, f, :]), f == 0, f == 1)
                        ins.then_inc(s_o[l], 1)

                def ffn_iter(it, first):
                    if first:
                        first_u_tiles()
                    else:
                        u_tile(it, 0, first)
                        u_tile(it, 1, first)
                    if first:
                        if l < DEPTH - 1:
                            mod_ffn(l, 0, 0)
                            mod_ffn(l, 0, 1)
                    else:
                        out_pass(it - 1)
                    u_tile(it, 2, first)
                    if l < DEPTH - 1:
                        mod_ffn_sum(l, it)
                    u_tile(it, 3, first)

                ffn_iter(0, True)
                ffn_iter(1, False)
                with pe.Fori(2, ITERS) as it:
                    ffn_iter(it, False)
                out_pass(ITERS - 1)
                if l < DEPTH - 1:
                    mod_ffn_sum(l, MOD_PASSES - 1)

        @block.scalar
        def _(act):
            own = Steps(act, s_act)

            def split_w(c, units, waits=None):
                for u in units:
                    if waits is not None:
                        act.wait_ge(s_wused, waits + u + 1)
                    act.wait_ge(s_w[u // 4], c * 16 + 16)
                    act.activation(w_hi[:, u, :], w_stage[:, u, :], ACT.Copy).then_inc(s_whi, 1)

            def square(n, d):
                l, second = n // 2, n % 2
                if n == 0:
                    act.wait_ge(s_x, 16)
                elif second:
                    act.wait_ge(s_mxadd[l], d + 1)
                    if d == 0 and l:
                        act.wait_ge(s_kv_out, 32 * l)
                else:
                    act.wait_ge(s_oadd[l - 1], KT * (ITERS - 1) + d + 1)
                if d >= 3:
                    act.wait_ge(s_sqsum, (KT - 1) * n + d - 2)
                dst = sq_sum if d == 0 else sq[d % 2]
                act.activation(dst[:, :], xT[:, d, :], ACT.Square).then_inc(s_sq, 1)

            def norm_act(n):
                l, second = n // 2, n % 2
                for d in range(KT - 1 if second and l else 0, KT):
                    square(n, d)
                b = MOD_SH2 if second else MOD_SH1
                for d in range(KT):
                    act.wait_ge(s_xs, KT * n + d + 1)
                    for i, (c, w) in enumerate(((CTX0, SEQ), (LAT0, DEC_SEQ))):
                        ins = act.activation(h_hi[:, d, c:c + w], xs[d % 2][:, c:c + w], ACT.Identity,
                                             bias=mod[l % 2][:, b + d, i:i + 1])
                        if i == 0:
                            own(ins)
                    ins.then_inc(s_hhi, 1)

            act.wait_ge(s_small, 32)
            act.wait_ge(s_pool, 2)
            act.activation(cond[:, :, 0:2], vec[:, V_COND:V_SUM].rearrange("p (k i) -> p k i", i=2),
                           ACT.Silu).then_inc(s_cond, 1)
            for l in range(DEPTH):
                norm_act(2 * l)
                c0 = FIRST_CHUNK[l]
                if l == 0:
                    split_w(0, range(UNITS))
                    for d in range(KT):
                        act.wait_ge(s_pool32, d + 1)
                        own(act.activation(h_hi[:, d, CTX0:CTX0 + SEQ], hp[2][:, PAD:PAD + SEQ], ACT.Copy))
                        act.activation(h_hi[:, d, LAT0:LAT0 + DEC_SEQ], hp[2][:, 2 * PAD + SEQ:2 * PAD + SEQ + DEC_SEQ],
                                       ACT.Copy).then_inc(s_pooled_hi, 1)
                    split_w(1, range(UNITS), waits=0)
                else:
                    nq = QKV_CHUNKS[l]
                    kv = qkv[nq]
                    normed = {(c, j): (i, n) for i, (c, j, n) in enumerate(NORMED[l])}
                    for c in range(nq):
                        for j in range(NT):
                            i = c * NT + j
                            if j == NT - 1 and c < nq - 1:
                                split_w(c0 + c + 1, range(UNITS), waits=UNITS * (c0 + c))
                            if j < NT - 1:
                                act.wait_ge(s_qp[l], c * (NT - 1) + j + 1)
                            else:
                                act.wait_ge(s_wused, UNITS * (c0 + c + 1))
                            ps = psA[:, i % 4, :]
                            if (c, j) in normed:
                                k, n = normed[c, j]
                                if k >= 2:
                                    act.wait_ge(s_qms[l], k - 1)
                                own(act.activation(qkv_sq[k % 2][:, 0:n * DH], ps[:, 0:n * DH], ACT.Square))
                            act.activation(kv[:, j, c * UNIT:(c + 1) * UNIT], ps, ACT.Copy).then_inc(s_qe[l], 1)
                    act.wait_ge(s_qkv, l)
                    (attention_diff_act if l == 2 else attention_act)(act, own, l)
                    cw = c0 + nq
                    act.wait_ge(s_att[l], ATT_DONE[l])
                    split_w(cw, range(UNITS))
                    for dt in range(KT):
                        split_w(cw + dt // 4 + 1, (2 * (dt % 4), 2 * (dt % 4) + 1), waits=UNITS * (cw + dt // 4))
                        if dt:
                            square(2 * l + 1, dt - 1)

                norm_act(2 * l + 1)
                cf = FFN_CHUNK[l]

                def evac(it, ft, first):
                    act.wait_ge(s_wused, it * UNITS + (UNITS * cf + 2 * ft + 2))
                    if not (first and ft < 2):
                        act.wait_ge(s_conv[l], it * 4 + (ft - 1))
                    act.activation(u_raw[ft % 2][:, :].rearrange("p (a n) -> p a n", a=2),
                                   psA[:, 2 * (ft % 2):2 * (ft % 2) + 2, 0:HALF], ACT.Copy).then_inc(s_u[l], 1)

                def split_next(it, ft):
                    for u in (2 * ft, 2 * ft + 1):
                        act.wait_ge(s_w[u // 4], it * 16 + 16 * (cf + 2))
                        act.activation(w_hi[:, u, :], w_stage[:, u, :], ACT.Copy).then_inc(s_whi, 1)

                def silu(it, p):
                    act.wait_ge(s_conv[l], it * 4 + (2 * p + 1))
                    act.activation(conv[0][:, 1:COLS - 1], conv[0][:, 1:COLS - 1], ACT.Silu).then_inc(s_silu[l], 1)

                def ghi(it, p):
                    act.wait_ge(s_gate[l], it * 2 + (p + 1))
                    act.activation(g_hi[:, p, 1:COLS - 1], conv[1][:, 1:COLS - 1], ACT.Copy).then_inc(s_ghi[l], 1)

                def ffn_iter(it, first, last):
                    for p in range(2):
                        evac(it, 2 * p, first)
                        if not last:
                            split_next(it, 2 * p)
                        evac(it, 2 * p + 1, first)
                        if not last:
                            split_next(it, 2 * p + 1)
                        silu(it, p)
                        if p == 0:
                            if not first:
                                act.wait_ge(s_o[l], it * KT)
                            act.wait_ge(s_wo, it * 16 + 16 * (ITERS * l + 1))
                            for f in range(2):
                                act.activation(wo_hi[:, f, :], wo_stage[:, f, :], ACT.Copy).then_inc(s_wohi, 1)
                        ghi(it, p)

                ffn_iter(0, True, False)
                ffn_iter(1, False, False)
                with act.Fori(2, ITERS - 1) as it:
                    ffn_iter(it, False, False)
                ffn_iter(ITERS - 1, False, l == DEPTH - 1)

        @block.vector
        def _(dve):
            own = Steps(dve, s_dve)

            def lo_w(u, value):
                dve.wait_ge(s_whi, value)
                dve.tensor_tensor(w_lo[:, u, :], w_stage[:, u, :], w_hi[:, u, :].bitcast(F32),
                                  ALU.subtract).then_inc(s_wlo, 1)

            def mod_bias(l, m, bank, count):
                dve.wait_ge(s_mod, count)
                if isinstance(m, int):
                    o = mod[l % 2][:, 4 * m:4 * m + 4, :]
                    b = vec[:, l * V_LAYER + V_BMOD + 4 * m:l * V_LAYER + V_BMOD + 4 * m + 4]
                else:
                    o = mod[l % 2][:, ds(m * 4, 4), :]
                    b = vec[:, ds(m * 4 + (l * V_LAYER + V_BMOD), 4)]
                dve.tensor_tensor(o, bank[:, MOD_AT:MOD_AT + 8].rearrange("p (a b) -> p a b", b=2),
                                  b.unsqueeze(2).to_broadcast([P, 4, 2]), ALU.add).then_inc(s_modok, 1)

            def mod_copy(m):
                dve.wait_ge(s_mraw, 2 * m + 2)
                if m:
                    dve.wait_ge(s_mod, m)
                dve.tensor_copy(mod_rows[:, :, :].rearrange("p a n -> p (a n)"), psA[:, m % 2, :]).then_inc(s_mrows, 1)

            def mod_first_bias(m):
                mod_bias(0, m, psA[:, 2 + m % 2, :], m + 1)

            def mod_copy_ffn(l, it, g):
                dve.wait_ge(s_mraw, it * 2 + (2 * MOD_PASSES * (l + 1) + g + 1))
                dve.wait_ge(s_mod, it + MOD_PASSES * (l + 1))
                dve.tensor_copy(mod_rows[:, 2 * g:2 * g + 2, :],
                                psB[:, 2 * g:2 * g + 2, 3 * P:4 * P]).then_inc(s_mrows, 1)

            def add_square(n, d):
                dve.wait_ge(s_sq, KT * n + d + 1)
                if d > 1:
                    dve.wait_ge(s_sqsum, (KT - 1) * n + d - 1)
                dve.tensor_tensor(sq_sum[:, :], sq_sum[:, :], sq[d % 2][:, :], ALU.add).then_inc(s_sqsum, 1)

            def norm_dve(n):
                l, second = n // 2, n % 2
                md = mod[l % 2]
                for d in range(1 if n < 2 else KT - 2, KT):
                    add_square(n, d)
                sc = MOD_SC2 if second else MOD_SC1
                v = l * V_LAYER + (V_N2 if second else V_N1)
                dve.wait_ge(s_modok, FIRST_PASSES if n == 0 else MOD_PASSES * (l + 1))
                own(dve.scalar_tensor_tensor(out=mod_a[:, :, :], in0=md[:, sc:sc + KT, :], scalar=1.0,
                                             in1=vec[:, v:v + KT].unsqueeze(2).to_broadcast([P, KT, 2]),
                                             op0=ALU.add, op1=ALU.mult))
                dve.wait_ge(s_stat, n + 1)
                dve.tensor_scalar(ms[:, :], psB[:, 0, 0:2 * NT].rearrange("p (j t) -> p j t", t=2)[:, :, 0],
                                  1.0 / D_MODEL, EPS, ALU.mult, ALU.add).then_inc(s_ms, 1)
                dve.wait_ge(s_rs, n + 1)
                dve.tensor_copy(rstd_rows[:, :, :], rs[:, :].unsqueeze(2).to_broadcast([P, NT, P])
                                ).then_inc(s_rows, 1)
                dve.wait_ge(s_bc, n + 1)
                own.wait()
                sh = MOD_SH2 if second else MOD_SH1
                parts = ((CTX0, SEQ, psB[:, 2, 0:P]), (LAT0, DEC_SEQ, psB[:, 3, :]))

                def scaled(d):
                    if d >= 2:
                        dve.wait_ge(s_h, KT * n + d - 1)
                    for i, (c, w, r) in enumerate(parts):
                        ins = dve.scalar_tensor_tensor(out=xs[d % 2][:, c:c + w], in0=xT[:, d, c:c + w],
                                                       scalar=mod_a[:, d, i:i + 1], in1=r,
                                                       op0=ALU.mult, op1=ALU.mult)
                        if i == 0:
                            own(ins)
                    ins.then_inc(s_xs, 1)

                def lo(d):
                    dve.wait_ge(s_hhi, KT * n + d + 1)
                    for i, (c, w, _) in enumerate(parts):
                        ins = dve.scalar_tensor_tensor(out=h_lo[:, d, c:c + w], in0=xs[d % 2][:, c:c + w],
                                                       scalar=md[:, sh + d, i:i + 1],
                                                       in1=h_hi[:, d, c:c + w].bitcast(F32),
                                                       op0=ALU.add, op1=ALU.subtract)
                        if i == 0:
                            own(ins)
                    ins.then_inc(s_h, 1)

                scaled(0)
                for d in range(KT):
                    if d + 1 < KT:
                        scaled(d + 1)
                    lo(d)

            def add_out(slot, d, gate, done):
                for c, w, i in ((CTX0, SEQ, 0), (LAT0, HALF - LAT0, 1), (HALF, LAT0 + DEC_SEQ - HALF, 1)):
                    bank = 2 * slot + (c >= HALF)
                    at_ = c % HALF
                    ins = dve.scalar_tensor_tensor(out=xT[:, d, c:c + w], in0=psB[:, bank, at_:at_ + w],
                                                   scalar=gate[:, d, i:i + 1], in1=xT[:, d, c:c + w],
                                                   op0=ALU.mult, op1=ALU.add)
                    if c < HALF:
                        own(ins)
                ins.then_inc(done, 1)

            own(dve.memset(ones2[:, :], 1.0))
            dve.memset(h_hi[:, :, :].bitcast(mybir.dt.uint32), 0).then_inc(s_const, 1)
            dve.memset(h_lo[:, :, :].bitcast(mybir.dt.uint32), 0).then_inc(s_const, 1)
            dve.wait_ge(s_const, 2)
            for m in range(FIRST_PASSES):
                mod_copy(m)
                if m:
                    mod_first_bias(m - 1)
            mod_first_bias(FIRST_PASSES - 1)

            for l in range(DEPTH):
                norm_dve(2 * l)
                c0 = FIRST_CHUNK[l]
                md = mod[l % 2]
                if l == 0:
                    for u in range(UNITS):
                        lo_w(u, u + 1)
                    pool_dve(dve, own, md, add_out, mod_copy, mod_first_bias)
                    for u in range(UNITS):
                        lo_w(u, UNITS + u + 1)
                else:
                    qkv_dve(dve, own, lo_w, l)
                    (attention_diff_dve if l == 2 else attention_dve)(dve, own, l)
                    cw = c0 + QKV_CHUNKS[l]
                    for u in range(UNITS):
                        lo_w(u, UNITS * cw + u + 1)
                    for dt in range(KT):
                        dve.wait_ge(s_wused, UNITS * (cw + dt // 4) + 2 * (dt % 4) + 2)
                        add_out(dt % 2, dt, md[:, MOD_G1:MOD_G1 + KT, :], s_mxadd[l])
                        for u in (2 * (dt % 4), 2 * (dt % 4) + 1):
                            lo_w(u, UNITS * (cw + dt // 4 + 1) + u + 1)
                        if dt > 2:
                            add_square(2 * l + 1, dt - 2)

                if l:
                    dve.wait_ge(s_kv_out, 32 * l)
                for b in (g_hi, g_lo):
                    own(dve.memset(b[:, :, 0:1].bitcast(mybir.dt.uint32), 0))
                    own(dve.memset(b[:, :, COLS - 2:COLS].bitcast(mybir.dt.uint32), 0))
                norm_dve(2 * l + 1)
                cf = FFN_CHUNK[l]
                def convolve(it, ft, between=(None, None)):
                    dve.wait_ge(s_u[l], it * 4 + (ft + 1))
                    u, o = u_raw[ft % 2], conv[ft % 2]
                    v = it * 16 + (l * V_LAYER + V_CONV + 4 * ft)
                    n = COLS - 2
                    own(dve.tensor_scalar(o[:, 1:1 + n], u[:, 1:1 + n], vcol(v + 1), vcol(v + 3), ALU.mult, ALU.add))
                    if between[0] is not None:
                        out_add(it - 1, between[0])
                    own.wait()
                    own(dve.scalar_tensor_tensor(out=o[:, 1:1 + n], in0=u[:, 0:n], scalar=vcol(v),
                                                 in1=o[:, 1:1 + n], op0=ALU.mult, op1=ALU.add))
                    if between[1] is not None:
                        out_add(it - 1, between[1])
                    own.wait()
                    dve.scalar_tensor_tensor(out=o[:, 1:1 + n], in0=u[:, 2:2 + n], scalar=vcol(v + 2),
                                             in1=o[:, 1:1 + n], op0=ALU.mult, op1=ALU.add).then_inc(s_conv[l], 1)

                def gate(it, p):
                    dve.wait_ge(s_silu[l], it * 2 + (p + 1))
                    dve.wait_ge(s_conv[l], it * 4 + (2 * p + 2))
                    dve.tensor_tensor(conv[1][:, 1:COLS - 1], conv[0][:, 1:COLS - 1], conv[1][:, 1:COLS - 1],
                                      ALU.mult).then_inc(s_gate[l], 1)

                def glo(it, p):
                    dve.wait_ge(s_gate[l], it * 2 + (p + 1))
                    dve.wait_ge(s_ghi[l], it * 2 + (p + 1))
                    dve.tensor_tensor(g_lo[:, p, 1:COLS - 1], conv[1][:, 1:COLS - 1],
                                      g_hi[:, p, 1:COLS - 1].bitcast(F32), ALU.subtract).then_inc(s_g[l], 1)

                def out_add(it, d):
                    dve.wait_ge(s_o[l], it * KT + (d + 1))
                    add_out(d % 2, d, md[:, MOD_G2:MOD_G2 + KT, :], s_oadd[l])

                def lo_next(it, ft):
                    for u in (2 * ft, 2 * ft + 1):
                        lo_w(u, it * UNITS + (UNITS * (cf + 1) + u + 1))

                def ffn_iter(it, first, last):
                    convolve(it, 0)
                    if not last:
                        lo_next(it, 0)
                    convolve(it, 1, (None, None) if first else (0, 1))
                    if not first:
                        out_add(it - 1, 2)
                    gate(it, 0)
                    if not first:
                        out_add(it - 1, 3)
                        out_add(it - 1, 4)
                    if not last:
                        lo_next(it, 1)
                    if not first:
                        for d in range(5, KT):
                            out_add(it - 1, d)
                            if d >= KT - 2 and l < DEPTH - 1:
                                mod_copy_ffn(l, it, d % 2)
                    elif l < DEPTH - 1:
                        mod_copy_ffn(l, 0, 0)
                        mod_copy_ffn(l, 0, 1)
                    for f in range(2):
                        dve.wait_ge(s_wohi, it * 2 + (2 * ITERS * l + f + 1))
                        dve.tensor_tensor(wo_lo[:, f, :], wo_stage[:, f, :], wo_hi[:, f, :].bitcast(F32),
                                          ALU.subtract).then_inc(s_wolo, 1)
                    glo(it, 0)
                    convolve(it, 2)
                    if not last:
                        lo_next(it, 2)
                    convolve(it, 3)
                    gate(it, 1)
                    if l < DEPTH - 1:
                        mod_bias(l + 1, it, psB[:, 3, :], it + (MOD_PASSES * (l + 1) + 1))
                    glo(it, 1)
                    if not last:
                        lo_next(it, 3)

                ffn_iter(0, True, False)
                ffn_iter(1, False, False)
                per = 4 * 2 + 2 * KT
                own_before = own.n
                with dve.Fori(2, ITERS - 1) as it:
                    own.loop = (it - 2) * per
                    ffn_iter(it, False, False)
                assert own.n - own_before == per
                own.loop = 0
                own.n = own_before + per * (ITERS - 3)
                ffn_iter(ITERS - 1, False, l == DEPTH - 1)
                for d in range(KT):
                    out_add(ITERS - 1, d)
                    if d >= KT - 2 and l < DEPTH - 1:
                        mod_copy_ffn(l, MOD_PASSES - 1, d % 2)
                    if d > 2 and l < DEPTH - 1:
                        add_square(2 * l + 2, d - 2)
                if l < DEPTH - 1:
                    mod_bias(l + 1, MOD_PASSES - 1, psB[:, 3, :], MOD_PASSES * (l + 2))



def _chunk(w):
    return w.reshape(KT, P, UNIT).transpose(1, 0, 2).reshape(P, -1)


def _tile_chunk(w):
    return w.reshape(KT, P, 4, P).transpose(1, 2, 0, 3).reshape(P, -1)


def _layout(x):
    weights = np.zeros((N_CHUNKS, P, UNITS * UNIT), np.float32)
    pool = weights[0].reshape(P, 4, 2, 2, 256)
    pool[:, :, :, 0, :] = x["pool_w"][0].reshape(4, 2, P, 256).transpose(2, 0, 1, 3)
    for l, name in ((1, "gqa"), (2, "diff"), (3, "win")):
        c = FIRST_CHUNK[l]
        for i in range(QKV_CHUNKS[l]):
            weights[c + i] = _chunk(x[f"{name}_w_qkv"][0][:, i * UNIT:(i + 1) * UNIT])
        for i in range(2):
            weights[c + QKV_CHUNKS[l] + i] = _tile_chunk(x[f"{name}_w_o"][0][:, i * UNIT:(i + 1) * UNIT])
    for l in range(DEPTH):
        w = x["ffn_w_in"][l].reshape(KT, P, 2, ITERS, 2, P).transpose(3, 1, 4, 2, 0, 5)
        weights[FFN_CHUNK[l]:FFN_CHUNK[l] + ITERS] = w.reshape(ITERS, P, -1)
    w_out = x["ffn_w_out"].reshape(DEPTH * ITERS, 2, P, D_MODEL).transpose(0, 2, 1, 3).reshape(DEPTH * ITERS, P, -1)
    w_mod = x["w_mod"].reshape(DEPTH, KT, P, MOD_PASSES, 2, 2 * P).transpose(0, 3, 2, 4, 1, 5)
    w_mod = w_mod.reshape(DEPTH * MOD_PASSES, P, 2, -1)

    vec = np.zeros((P, V_ALL), np.float32)
    for l in range(DEPTH):
        v = l * V_LAYER
        vec[:, v + V_BMOD:v + V_N1] = x["b_mod"][l].reshape(48, P).T
        vec[:, v + V_N1:v + V_N2] = x["norm1_g"][l].reshape(KT, P).T
        vec[:, v + V_N2:v + V_CONV] = x["norm2_g"][l].reshape(KT, P).T
        taps = np.concatenate([x["ffn_conv_w"][l], x["ffn_conv_b"][l][None]])
        taps = taps.reshape(4, 2, ITERS, 2, P).transpose(4, 2, 3, 1, 0)
        vec[:, v + V_CONV:v + V_LAYER] = taps.reshape(P, -1)
    vec[:, V_POOL:V_COND] = x["pool_scale"][0].reshape(KT, P).T
    both = np.stack([x["c_ctx"], x["c"][0]])
    vec[:, V_COND:V_SUM] = both.reshape(2, KT, P).transpose(2, 1, 0).reshape(P, -1)
    vec[np.arange(0, P, 32), V_SUM] = 1.0
    vec[np.arange(1, P, 32), V_SUM + 1] = 1.0

    rows = [x[f"{n}_q_norm"][0] for n in ("gqa", "diff", "win")] + [x[f"{n}_k_norm"][0] for n in ("gqa", "diff", "win")]
    rows += [x["diff_sub_norm"][0]] + [x[f"diff_lambda_{n}"][0] for n in ("q1", "k1", "q2", "k2")] + [x["win_sink"][0]]
    row = np.broadcast_to(np.concatenate(rows), (P, R_ALL))

    xT = np.zeros((P, KT, COLS), np.float32)
    xT[:, :, CTX0:CTX0 + SEQ] = x["x_prompt"][0].reshape(SEQ, KT, P).transpose(2, 1, 0)
    xT[:, :, LAT0:LAT0 + DEC_SEQ] = x["x_sample"][0].reshape(DEC_SEQ, KT, P).transpose(2, 1, 0)

    pos = np.arange(DEC_SEQ)
    inv = np.float32(THETA) ** (-np.arange(0, DH // 2, 2, dtype=np.float32) / np.float32(DH // 2))
    angle = np.stack([(pos // GRID_W).astype(np.float32)[:, None] * inv,
                      (pos % GRID_W).astype(np.float32)[:, None] * inv], axis=1)
    cos, sin = np.cos(angle), np.sin(angle)
    rope = np.stack([np.stack([cos, cos], 2), np.stack([-sin, sin], 2)]).reshape(2, NT - 1, P, DH)
    counts = []
    for w in POOL_WINDOWS:
        for n in (SEQ, DEC_SEQ):
            at = np.arange(n)
            counts.append(1.0 / (np.clip(at - w // 2 + w, 0, n) - np.clip(at - w // 2, 0, n)))
    inv_count = np.broadcast_to(np.concatenate(counts).astype(np.float32), (P, 4 * (SEQ + DEC_SEQ)))
    q, k = np.arange(P)[:, None], np.arange(P)[None, :]
    mask = np.stack([np.where(k >= q, 0.0, NEG), np.where(k <= q, 0.0, NEG)], 1)

    arrays = {
        "weights": weights, "w_out": w_out, "w_mod": w_mod, "vec": vec, "row": row,
        "xT": xT.reshape(P, -1), "ident": np.eye(P, dtype=np.float32),
        "rope": rope.transpose(2, 0, 1, 3).reshape(P, -1).astype(np.float32),
        "inv_count": inv_count, "mask": mask.reshape(P, -1).astype(np.float32),
    }
    for l, name in ((1, "gqa"), (2, "diff"), (3, "win")):
        arrays[f"ck{l}"] = x[f"cache_{name}_k"][0, 0].reshape(PAST, -1)
        arrays[f"cv{l}"] = x[f"cache_{name}_v"][0, 0].reshape(PAST, -1)
    return {n: np.ascontiguousarray(a) for n, a in arrays.items()}


def kernel(**inputs):
    import concourse.bacc as bacc
    from concourse.bass_utils import run_bass_kernel_spmd

    nc = bacc.Bacc("TRN2", target_bir_lowering=False, num_devices=1)
    arrays = _layout({n: np.asarray(a) for n, a in inputs.items()})
    tensors = {}
    for name, a in arrays.items():
        tensors[name] = nc.dram_tensor(f"{name}_dram", a.shape, F32, kind="ExternalInput").ap()
    outs = {"yT": (P, KT * COLS)}
    for l in (1, 2, 3):
        for n in "kv":
            outs[f"{n}{l}"] = (SEQ, D_MODEL if l == 2 else KV_HEADS * DH)
    for name, shape in outs.items():
        tensors[name] = nc.dram_tensor(f"{name}_dram", shape, F32, kind="ExternalOutput").ap()
    program(nc, tensors)
    r = run_bass_kernel_spmd(nc, [{f"{n}_dram": a for n, a in arrays.items()}], core_ids=[0])
    got = {name: r.results[0][f"{name}_dram"] for name in outs}
    y = got["yT"].reshape(P, KT, COLS).transpose(2, 1, 0).reshape(COLS, D_MODEL)
    y_prompt, y_sample = y[CTX0:CTX0 + SEQ][None], y[LAT0:LAT0 + DEC_SEQ][None]
    kv = (1, 1, SEQ, KV_HEADS, DH)
    return (np.ascontiguousarray(y_prompt), np.ascontiguousarray(y_sample),
            got["k1"].reshape(kv), got["v1"].reshape(kv),
            got["k2"].reshape(1, 1, SEQ, DIFF_HEADS, 2, DH), got["v2"].reshape(1, 1, SEQ, DIFF_HEADS, 2 * DH),
            got["k3"].reshape(kv), got["v3"].reshape(kv))
```
